# Optimizing a Trainium2 kernel written in Bass

```python
import math
import jax, jax.numpy as jnp
from jax import lax
import numpy as np

D_MODEL = 1024
BATCH = 1
SEQ = 512
DEPTH = 2

BLOCK = 128
EPS = 1e-6
HEAD_DIM = 64
SB_HEADS = 8
SW_HEADS = 8
SW_KV_HEADS = 2
SW_GROUP = SW_HEADS // SW_KV_HEADS
WINDOW = 128
SB_WIDTH = SB_HEADS * HEAD_DIM
SW_Q_WIDTH = SW_HEADS * HEAD_DIM
SW_KV_WIDTH = SW_KV_HEADS * HEAD_DIM
EVEN_SPLITS = [SB_WIDTH, SB_WIDTH, SB_WIDTH, SW_Q_WIDTH, SW_KV_WIDTH, SW_KV_WIDTH]
EVEN_IN_WIDTH = sum(EVEN_SPLITS)
EVEN_OUT_WIDTH = SB_WIDTH + SW_Q_WIDTH
REL_BUCKETS = 32
REL_MAX_DIST = 128
MLA_HEADS = 16
MLA_NOPE_DIM = 64
MLA_ROPE_DIM = 32
MLA_V_DIM = 64
MLA_Q_RANK = 384
MLA_KV_RANK = 256
MLA_DOWN_WIDTH = MLA_Q_RANK + MLA_KV_RANK + MLA_ROPE_DIM
ROPE_THETA = 10000.0
FFN_HIDDEN = -(-8 * D_MODEL // (3 * 256)) * 256
N_EVEN = (DEPTH + 1) // 2
N_ODD = DEPTH // 2


F32 = jnp.float32

def rmsnorm(x, g):
    xf = x.astype(F32)
    y = xf * lax.rsqrt(jnp.mean(xf * xf, axis=-1, keepdims=True) + EPS)
    return (y * g.astype(F32)).astype(x.dtype)

def t5_bucket(rel):
    max_exact = REL_BUCKETS // 2
    rel = jnp.maximum(rel, 0)
    relf = jnp.maximum(rel, 1).astype(F32)
    large = max_exact + (jnp.log(relf / max_exact) / math.log(REL_MAX_DIST / max_exact)
                         * (REL_BUCKETS - max_exact)).astype(jnp.int32)
    large = jnp.minimum(large, REL_BUCKETS - 1)
    return jnp.where(rel < max_exact, rel, large)

def stick_breaking_attention(q, k, v):
    B_, S, H, d = q.shape
    nb = S // BLOCK
    scale = d ** -0.5
    qb = q.reshape(B_, nb, BLOCK, H, d).transpose(1, 0, 3, 2, 4)
    key_pos = jnp.arange(S)

    def one_block(args):
        q_blk, i = args
        z = jnp.einsum('bhqd,bshd->bhqs', q_blk, k, preferred_element_type=F32) * scale
        q_pos = i * BLOCK + jnp.arange(BLOCK)
        causal = key_pos[None, :] < q_pos[:, None]
        log_beta = jax.nn.log_sigmoid(z)
        log_1m_beta = jnp.where(causal, jax.nn.log_sigmoid(-z), 0.0)
        between = lax.cumsum(log_1m_beta, axis=3, reverse=True) - log_1m_beta
        w = jnp.where(causal, jnp.exp(log_beta + between), 0.0)
        return jnp.einsum('bhqs,bshd->bqhd', w.astype(v.dtype), v)

    out = lax.map(one_block, (qb, jnp.arange(nb)))
    return out.transpose(1, 0, 2, 3, 4).reshape(B_, S, H * d)

def sliding_window_attention(q, k, v, sinks, rel_bias_table):
    B_, S, Hq, d = q.shape
    Hkv = k.shape[2]
    G = Hq // Hkv
    nb = S // BLOCK
    qb = q.reshape(B_, nb, BLOCK, Hkv, G, d)

    def banded(t):
        tb = t.reshape(B_, nb, BLOCK, Hkv, d)
        prev = jnp.concatenate([jnp.zeros_like(tb[:, :1]), tb[:, :-1]], axis=1)
        return jnp.concatenate([prev, tb], axis=2)

    kb, vb = banded(k), banded(v)
    logits = jnp.einsum('bnqkgd,bnskd->bnkgqs', qb, kb, preferred_element_type=F32) * d ** -0.5
    rel = BLOCK + jnp.arange(BLOCK)[:, None] - jnp.arange(2 * BLOCK)[None, :]
    in_window = (rel >= 0) & (rel < WINDOW)
    key_pos = (jnp.arange(nb)[:, None] - 1) * BLOCK + jnp.arange(2 * BLOCK)[None, :]
    valid = in_window[None] & (key_pos >= 0)[:, None, :]
    bias = rel_bias_table.astype(F32)[t5_bucket(rel)]
    bias = bias.transpose(2, 0, 1).reshape(Hkv, G, BLOCK, 2 * BLOCK)
    logits = jnp.where(valid[None, :, None, None], logits + bias, -jnp.inf)
    sink = sinks.astype(F32).reshape(Hkv, G)[:, :, None, None]
    m = jnp.maximum(jnp.max(logits, axis=-1, keepdims=True), sink)
    p = jnp.exp(logits - m)
    p = p / (jnp.sum(p, axis=-1, keepdims=True) + jnp.exp(sink - m))
    out = jnp.einsum('bnkgqs,bnskd->bnqkgd', p.astype(v.dtype), vb)
    return out.reshape(B_, S, Hq * d)

def rope(x, positions):
    half = x.shape[-1] // 2
    freqs = ROPE_THETA ** (-jnp.arange(half, dtype=F32) / half)
    ang = positions.astype(F32)[..., None] * freqs
    cos = jnp.cos(ang)[:, :, None, :]
    sin = jnp.sin(ang)[:, :, None, :]
    x1 = x[..., :half].astype(F32)
    x2 = x[..., half:].astype(F32)
    return jnp.concatenate([x1 * cos - x2 * sin, x2 * cos + x1 * sin], axis=-1).astype(x.dtype)

def mla_attention(q_nope, q_rope, k_nope, k_rope, v):
    B_, S, H, _ = q_nope.shape
    nb = S // BLOCK
    scale = (MLA_NOPE_DIM + MLA_ROPE_DIM) ** -0.5
    qn = q_nope.reshape(B_, nb, BLOCK, H, MLA_NOPE_DIM).transpose(1, 0, 2, 3, 4)
    qr = q_rope.reshape(B_, nb, BLOCK, H, MLA_ROPE_DIM).transpose(1, 0, 2, 3, 4)
    key_pos = jnp.arange(S)

    def one_block(args):
        qn_blk, qr_blk, i = args
        s = (jnp.einsum('bqhd,bshd->bhqs', qn_blk, k_nope, preferred_element_type=F32)
             + jnp.einsum('bqhr,bsr->bhqs', qr_blk, k_rope, preferred_element_type=F32)) * scale
        q_pos = i * BLOCK + jnp.arange(BLOCK)
        s = jnp.where(key_pos[None, :] <= q_pos[:, None], s, -jnp.inf)
        p = jax.nn.softmax(s, axis=-1)
        return jnp.einsum('bhqs,bshd->bqhd', p.astype(v.dtype), v)

    out = lax.map(one_block, (qn, qr, jnp.arange(nb)))
    return out.transpose(1, 0, 2, 3, 4).reshape(B_, S, H * MLA_V_DIM)

def even_mixer(h, w_in, sinks, rel_bias_table, w_out):
    B_, S, _ = h.shape
    proj = h @ w_in
    q_a, k_a, v_a, q_b, k_b, v_b = jnp.split(proj, list(np.cumsum(EVEN_SPLITS)[:-1]), axis=-1)
    hd = lambda t, n: t.reshape(B_, S, n, HEAD_DIM)
    o_a = stick_breaking_attention(hd(q_a, SB_HEADS), hd(k_a, SB_HEADS), hd(v_a, SB_HEADS))
    o_b = sliding_window_attention(hd(q_b, SW_HEADS), hd(k_b, SW_KV_HEADS), hd(v_b, SW_KV_HEADS),
                                   sinks, rel_bias_table)
    return jnp.concatenate([o_a, o_b], axis=-1) @ w_out

def mla_mixer(h, positions, w_down, q_norm, w_uq, kv_norm, w_ukv, w_o):
    B_, S, _ = h.shape
    down = h @ w_down
    c_q = down[..., :MLA_Q_RANK]
    c_kv = down[..., MLA_Q_RANK:MLA_Q_RANK + MLA_KV_RANK]
    k_rope = down[..., MLA_Q_RANK + MLA_KV_RANK:]
    q = (rmsnorm(c_q, q_norm) @ w_uq).reshape(B_, S, MLA_HEADS, MLA_NOPE_DIM + MLA_ROPE_DIM)
    q_nope = q[..., :MLA_NOPE_DIM]
    q_rope = rope(q[..., MLA_NOPE_DIM:], positions)
    kv = (rmsnorm(c_kv, kv_norm) @ w_ukv).reshape(B_, S, MLA_HEADS, MLA_NOPE_DIM + MLA_V_DIM)
    k_nope = kv[..., :MLA_NOPE_DIM]
    v = kv[..., MLA_NOPE_DIM:]
    k_rope = rope(k_rope[:, :, None, :], positions)[:, :, 0, :]
    return mla_attention(q_nope, q_rope, k_nope, k_rope, v) @ w_o

def swiglu(h, w_gate, w_up, w_down):
    return (jax.nn.silu(h @ w_gate) * (h @ w_up)) @ w_down

def first_inputs(seed: int = 0) -> dict:
    key = jax.random.key(seed)
    ks = jax.random.split(key, 20)
    nrm = lambda k, shape, fan_in: jax.random.normal(k, shape, F32) * fan_in ** -0.5
    gain = lambda k, shape: 1.0 + 0.02 * jax.random.normal(k, shape, F32)
    x = jax.random.normal(ks[0], (BATCH, SEQ, D_MODEL), F32)
    offsets = jax.random.randint(ks[1], (BATCH, 1), 0, 1024, dtype=jnp.int32)
    positions = (jnp.arange(SEQ, dtype=jnp.int32)[None, :] + offsets).astype(jnp.int32)
    return {
        "x": x,
        "positions": positions,
        "attn_norm": gain(ks[2], (DEPTH, D_MODEL)),
        "ffn_norm": gain(ks[3], (DEPTH, D_MODEL)),
        "even_w_in": nrm(ks[4], (N_EVEN, D_MODEL, EVEN_IN_WIDTH), D_MODEL),
        "even_sinks": 0.5 * jax.random.normal(ks[5], (N_EVEN, SW_HEADS), F32),
        "even_w_out": nrm(ks[6], (N_EVEN, EVEN_OUT_WIDTH, D_MODEL), EVEN_OUT_WIDTH),
        "rel_bias_table": 0.5 * jax.random.normal(ks[7], (REL_BUCKETS, SW_HEADS), F32),
        "mla_w_down": nrm(ks[8], (N_ODD, D_MODEL, MLA_DOWN_WIDTH), D_MODEL),
        "mla_q_norm": gain(ks[9], (N_ODD, MLA_Q_RANK)),
        "mla_w_uq": nrm(ks[10], (N_ODD, MLA_Q_RANK, MLA_HEADS * (MLA_NOPE_DIM + MLA_ROPE_DIM)), MLA_Q_RANK),
        "mla_kv_norm": gain(ks[11], (N_ODD, MLA_KV_RANK)),
        "mla_w_ukv": nrm(ks[12], (N_ODD, MLA_KV_RANK, MLA_HEADS * (MLA_NOPE_DIM + MLA_V_DIM)), MLA_KV_RANK),
        "mla_w_o": nrm(ks[13], (N_ODD, MLA_HEADS * MLA_V_DIM, D_MODEL), MLA_HEADS * MLA_V_DIM),
        "ffn_w_gate": nrm(ks[14], (DEPTH, D_MODEL, FFN_HIDDEN), D_MODEL),
        "ffn_w_up": nrm(ks[15], (DEPTH, D_MODEL, FFN_HIDDEN), D_MODEL),
        "ffn_w_down": nrm(ks[16], (DEPTH, FFN_HIDDEN, D_MODEL), FFN_HIDDEN),
        "final_norm": gain(ks[17], (D_MODEL,)),
    }

def first_block(x, positions, attn_norm, ffn_norm, even_w_in, even_sinks, even_w_out, rel_bias_table,
              mla_w_down, mla_q_norm, mla_w_uq, mla_kv_norm, mla_w_ukv, mla_w_o,
              ffn_w_gate, ffn_w_up, ffn_w_down, final_norm):
    for layer in range(DEPTH):
        h = rmsnorm(x, attn_norm[layer])
        if layer % 2 == 0:
            e = layer // 2
            x = x + even_mixer(h, even_w_in[e], even_sinks[e], rel_bias_table, even_w_out[e])
        else:
            o = layer // 2
            x = x + mla_mixer(h, positions, mla_w_down[o], mla_q_norm[o], mla_w_uq[o],
                              mla_kv_norm[o], mla_w_ukv[o], mla_w_o[o])
        h = rmsnorm(x, ffn_norm[layer])
        x = x + swiglu(h, ffn_w_gate[layer], ffn_w_up[layer], ffn_w_down[layer])
    return rmsnorm(x, final_norm)


DEPTH_2 = 1

MIX_DIM = D_MODEL
RWKV_HEADS = 8
RWKV_HEAD_DIM = 64
RWKV_DIM = RWKV_HEADS * RWKV_HEAD_DIM
LORA_W = 64
LORA_A = 64
LORA_G = 128
DIFF_HEADS = 4
DIFF_HEAD_DIM = 64
DIFF_DIM = DIFF_HEADS * 2 * DIFF_HEAD_DIM
RWKV_COLS = 3 * RWKV_DIM + LORA_W + LORA_A + LORA_G
DIFF_COLS = 3 * DIFF_DIM
IN_COLS = RWKV_COLS + DIFF_COLS
Q_BLOCK = 128
D_FF = 2816
CONV_WIDTH = 3
DECAY_SCALE = math.exp(-0.5)
RWKV_LN_EPS = 64e-5
NORM_EPS = 1e-6
SUBLN_EPS = 1e-5
NEG_INF = -1e30


def rms_norm(x, g, eps=NORM_EPS):
    x32 = x.astype(jnp.float32)
    y = x32 * lax.rsqrt(jnp.mean(x32 * x32, axis=-1, keepdims=True) + eps)
    return (y * g.astype(jnp.float32)).astype(x.dtype)

def alibi_slopes(n):
    return jnp.array([2.0 ** (-8.0 * (i + 1) / n) for i in range(n)], jnp.float32)

def token_shift(p):
    return jnp.pad(p[:, :-1], ((0, 0), (1, 0), (0, 0)))

def rwkv7_mix(p, mu, w_decay_up, w_decay0, w_iclr_up, w_iclr0, w_gate_up,
              k_k, k_a, r_k, ln_x_w, ln_x_b):
    B, S, _ = p.shape
    p = p.astype(jnp.float32)
    xs = p + (token_shift(p) - p) * mu
    cuts = [RWKV_DIM, 2 * RWKV_DIM, 3 * RWKV_DIM, 3 * RWKV_DIM + LORA_W,
            3 * RWKV_DIM + LORA_W + LORA_A]
    r, k, v, w_lo, a_lo, g_lo = jnp.split(xs, cuts, axis=-1)
    decay = jnp.exp(-DECAY_SCALE * jax.nn.sigmoid(w_decay0 + jnp.tanh(w_lo) @ w_decay_up))
    a = jax.nn.sigmoid(w_iclr0 + a_lo @ w_iclr_up)
    g = jax.nn.sigmoid(g_lo) @ w_gate_up
    hs = (B, S, RWKV_HEADS, RWKV_HEAD_DIM)
    kk = (k * k_k).reshape(hs)
    kk = kk / jnp.maximum(jnp.linalg.norm(kk, axis=-1, keepdims=True), 1e-12)
    k = k * (1.0 + (a - 1.0) * k_a)
    r, k, v, decay, a = (t.reshape(hs) for t in (r, k, v, decay, a))

    def step(state, inp):
        r_t, w_t, k_t, v_t, kk_t, a_t = inp
        sa = jnp.einsum('bhvk,bhk->bhv', state, -kk_t)
        state = (state * w_t[:, :, None, :]
                 + sa[..., None] * (kk_t * a_t)[:, :, None, :]
                 + v_t[..., None] * k_t[:, :, None, :])
        return state, jnp.einsum('bhvk,bhk->bhv', state, r_t)

    seq_major = tuple(jnp.moveaxis(t, 1, 0) for t in (r, decay, k, v, kk, a))
    s0 = jnp.zeros((B, RWKV_HEADS, RWKV_HEAD_DIM, RWKV_HEAD_DIM), jnp.float32)
    _, y = lax.scan(step, s0, seq_major)
    y = jnp.moveaxis(y, 0, 1)
    y = y + jnp.sum(r * k * r_k, axis=-1, keepdims=True) * v
    mean = jnp.mean(y, axis=-1, keepdims=True)
    var = jnp.mean(jnp.square(y - mean), axis=-1, keepdims=True)
    y = ((y - mean) * lax.rsqrt(var + RWKV_LN_EPS)).reshape(B, S, RWKV_DIM)
    y = y * ln_x_w + ln_x_b
    return y * g

def diff_attention(q, k, v, lam, slopes):
    B, S, H, _, d = q.shape
    nb = S // Q_BLOCK
    scale = d ** -0.5
    qh = q.transpose(0, 2, 3, 1, 4)
    kh = k.transpose(0, 2, 3, 1, 4).astype(jnp.float32)
    vh = v.transpose(0, 2, 1, 3).astype(jnp.float32)
    qb = qh.reshape(B, H, 2, nb, Q_BLOCK, d).transpose(3, 0, 1, 2, 4, 5)
    kpos = jnp.arange(S)

    def block(args):
        qblk, i = args
        qpos = i * Q_BLOCK + jnp.arange(Q_BLOCK)
        dist = (qpos[:, None] - kpos[None, :]).astype(jnp.float32)
        s = jnp.einsum('bhcqd,bhckd->bhcqk', qblk.astype(jnp.float32), kh) * scale
        s = s - slopes[None, :, None, None, None] * dist
        s = jnp.where(dist >= 0, s, NEG_INF)
        pr = jax.nn.softmax(s, axis=-1)
        attn = pr[:, :, 0] - lam * pr[:, :, 1]
        return jnp.einsum('bhqk,bhkv->bhqv', attn, vh)

    out = lax.map(block, (qb, jnp.arange(nb)))
    return out.transpose(1, 0, 3, 2, 4).reshape(B, S, H, 2 * d)

def causal_dwconv(h, w, b):
    C = h.shape[-1]
    y = lax.conv_general_dilated(h, w[:, None, :].astype(h.dtype), window_strides=(1,),
                                 padding=((CONV_WIDTH - 1, 0),),
                                 dimension_numbers=('NWC', 'WIO', 'NWC'),
                                 feature_group_count=C)
    return y + b.astype(h.dtype)

def second_inputs(seed: int = 0) -> dict:
    key = jax.random.key(seed)
    ks = jax.random.split(key, 32)
    L = DEPTH_2

    def nrm(k, shape, s):
        return jax.random.normal(k, shape, jnp.float32) * s

    return {
        "x": nrm(ks[0], (BATCH, SEQ, D_MODEL), 1.0),
        "ln_attn_pre": 1.0 + nrm(ks[1], (L, D_MODEL), 0.05),
        "w_in": nrm(ks[2], (L, D_MODEL, IN_COLS), D_MODEL ** -0.5),
        "mu_shift": jax.random.uniform(ks[3], (L, RWKV_COLS), jnp.float32),
        "w_decay_up": nrm(ks[4], (L, LORA_W, RWKV_DIM), LORA_W ** -0.5),
        "w_decay0": nrm(ks[5], (L, RWKV_DIM), 0.5),
        "w_iclr_up": nrm(ks[6], (L, LORA_A, RWKV_DIM), LORA_A ** -0.5),
        "w_iclr0": nrm(ks[7], (L, RWKV_DIM), 0.1),
        "w_gate_up": nrm(ks[8], (L, LORA_G, RWKV_DIM), LORA_G ** -0.5),
        "k_k": 0.85 + nrm(ks[9], (L, RWKV_DIM), 0.05),
        "k_a": 1.0 + nrm(ks[10], (L, RWKV_DIM), 0.05),
        "r_k": nrm(ks[11], (L, RWKV_HEADS, RWKV_HEAD_DIM), 0.1),
        "ln_x_w": 1.0 + nrm(ks[12], (L, RWKV_DIM), 0.05),
        "ln_x_b": nrm(ks[13], (L, RWKV_DIM), 0.02),
        "lambda_q1": nrm(ks[14], (L, DIFF_HEAD_DIM), 0.1),
        "lambda_k1": nrm(ks[15], (L, DIFF_HEAD_DIM), 0.1),
        "lambda_q2": nrm(ks[16], (L, DIFF_HEAD_DIM), 0.1),
        "lambda_k2": nrm(ks[17], (L, DIFF_HEAD_DIM), 0.1),
        "diff_subln": 1.0 + nrm(ks[18], (L, 2 * DIFF_HEAD_DIM), 0.05),
        "w_out": nrm(ks[19], (L, MIX_DIM, D_MODEL), MIX_DIM ** -0.5),
        "ln_attn_post": 1.0 + nrm(ks[20], (L, D_MODEL), 0.05),
        "ln_ffn_pre": 1.0 + nrm(ks[21], (L, D_MODEL), 0.05),
        "w_up": nrm(ks[22], (L, D_MODEL, 2 * D_FF), D_MODEL ** -0.5),
        "conv_w": nrm(ks[23], (L, CONV_WIDTH, 2 * D_FF), CONV_WIDTH ** -0.5),
        "conv_b": nrm(ks[24], (L, 2 * D_FF), 0.02),
        "w_down": nrm(ks[25], (L, D_FF, D_MODEL), D_FF ** -0.5),
        "ln_ffn_post": 1.0 + nrm(ks[26], (L, D_MODEL), 0.05),
    }

def second_block(x, ln_attn_pre, w_in, mu_shift, w_decay_up, w_decay0, w_iclr_up, w_iclr0,
              w_gate_up, k_k, k_a, r_k, ln_x_w, ln_x_b, lambda_q1, lambda_k1, lambda_q2,
              lambda_k2, diff_subln, w_out, ln_attn_post, ln_ffn_pre, w_up, conv_w, conv_b,
              w_down, ln_ffn_post):
    B, S, _ = x.shape
    slopes = alibi_slopes(DIFF_HEADS)
    h = x
    for l in range(DEPTH_2):
        xn = rms_norm(h, ln_attn_pre[l])
        proj = xn @ w_in[l]
        y_rwkv = rwkv7_mix(proj[..., :RWKV_COLS], mu_shift[l], w_decay_up[l], w_decay0[l],
                           w_iclr_up[l], w_iclr0[l], w_gate_up[l], k_k[l], k_a[l], r_k[l],
                           ln_x_w[l], ln_x_b[l])
        dq, dk, dv = jnp.split(proj[..., RWKV_COLS:], 3, axis=-1)
        dq = dq.reshape(B, S, DIFF_HEADS, 2, DIFF_HEAD_DIM)
        dk = dk.reshape(B, S, DIFF_HEADS, 2, DIFF_HEAD_DIM)
        dv = dv.reshape(B, S, DIFF_HEADS, 2 * DIFF_HEAD_DIM)
        lam_init = 0.8 - 0.6 * math.exp(-0.3 * l)
        lam = (jnp.exp(jnp.sum(lambda_q1[l] * lambda_k1[l]).astype(jnp.float32))
               - jnp.exp(jnp.sum(lambda_q2[l] * lambda_k2[l]).astype(jnp.float32)) + lam_init)
        o = diff_attention(dq, dk, dv, lam, slopes)
        o = rms_norm(o, diff_subln[l], eps=SUBLN_EPS) * (1.0 - lam_init)
        mix = jnp.concatenate([y_rwkv, o.reshape(B, S, DIFF_DIM)], axis=-1).astype(h.dtype)
        h = h + rms_norm(mix @ w_out[l], ln_attn_post[l])
        hn = rms_norm(h, ln_ffn_pre[l])
        u = causal_dwconv(hn @ w_up[l], conv_w[l], conv_b[l])
        gate, val = jnp.split(u, 2, axis=-1)
        f = (jax.nn.gelu(gate, approximate=True) * val) @ w_down[l]
        h = h + rms_norm(f, ln_ffn_post[l])
    return h


def setup_inputs(seed=0):
    out = dict(first_inputs(seed))
    for name, value in second_inputs(seed + 1).items():
        if name != "x":
            out[name + "_2"] = value
    return out


def reference(
    x, positions, attn_norm, ffn_norm, even_w_in, even_sinks, even_w_out, rel_bias_table,
    mla_w_down, mla_q_norm, mla_w_uq, mla_kv_norm, mla_w_ukv, mla_w_o, ffn_w_gate, ffn_w_up,
    ffn_w_down, final_norm, ln_attn_pre_2, w_in_2, mu_shift_2, w_decay_up_2, w_decay0_2,
    w_iclr_up_2, w_iclr0_2, w_gate_up_2, k_k_2, k_a_2, r_k_2, ln_x_w_2, ln_x_b_2, lambda_q1_2,
    lambda_k1_2, lambda_q2_2, lambda_k2_2, diff_subln_2, w_out_2, ln_attn_post_2, ln_ffn_pre_2,
    w_up_2, conv_w_2, conv_b_2, w_down_2, ln_ffn_post_2,
):
    x = first_block(
        x, positions, attn_norm, ffn_norm, even_w_in, even_sinks, even_w_out, rel_bias_table,
        mla_w_down, mla_q_norm, mla_w_uq, mla_kv_norm, mla_w_ukv, mla_w_o, ffn_w_gate, ffn_w_up,
        ffn_w_down, final_norm,
    )
    return second_block(
        x, ln_attn_pre_2, w_in_2, mu_shift_2, w_decay_up_2, w_decay0_2, w_iclr_up_2, w_iclr0_2,
        w_gate_up_2, k_k_2, k_a_2, r_k_2, ln_x_w_2, ln_x_b_2, lambda_q1_2, lambda_k1_2,
        lambda_q2_2, lambda_k2_2, diff_subln_2, w_out_2, ln_attn_post_2, ln_ffn_pre_2, w_up_2,
        conv_w_2, conv_b_2, w_down_2, ln_ffn_post_2,
    )


_drawn_inputs = setup_inputs


def setup_inputs(seed=0):
    import zlib

    import numpy as np

    out = dict(_drawn_inputs(seed))
    spreads = {}
    factors = {'even_sinks': 2.958,
     'mla_q_norm': 8.0,
     'mla_kv_norm': 7.014,
     'k_k_2': 8.0,
     'ln_x_b_2': 5.959,
     'lambda_q1_2': 4.301,
     'lambda_k1_2': 4.157,
     'lambda_q2_2': 5.789,
     'conv_b_2': 3.486}
    for name, (base, spread) in spreads.items():
        noise = np.random.default_rng([zlib.crc32(name.encode()), seed]).standard_normal(out[name].shape)
        drawn = base * np.exp(spread * noise) if base else spread * noise
        out[name] = __import__('jax').numpy.asarray(drawn.astype(out[name].dtype))
    for name, factor in factors.items():
        out[name] = (out[name] * factor).astype(out[name].dtype)
    return out
```

```python
from contextlib import ExitStack
import math

import numpy as np

import concourse.bass as bass
from concourse import mybir

F32 = mybir.dt.float32
F32R = mybir.dt.float32r
I32 = mybir.dt.int32
ACT = mybir.ActivationFunctionType
ALU = mybir.AluOpType
AX = mybir.AxisListType

P = 128
SEQ = 512
D = 1024
KT = D // P
ST = SEQ // P
HID = 2816
HT = HID // P
NEG = -1e30
EPS = 1e-6
SUBLN_EPS = 1e-5
RWKV_LN_EPS = 64e-5
DS = math.exp(-0.5)
CH = 128
NCH = SEQ // CH
LAM_INIT = 0.8 - 0.6
LEVELS = 7
UW = 2048

CONST_COLS = {}


def constants():
    q = np.arange(P)[:, None]
    k = np.arange(P)[None, :]
    cols = []

    def put(name, a):
        full = np.zeros((P, a.shape[1]), np.float32)
        full[: a.shape[0]] = a
        at = sum(c.shape[1] for c in cols)
        CONST_COLS[name] = (at, a.shape[1])
        cols.append(full)

    put("ident", np.eye(P, dtype=np.float32))
    put("flip", np.eye(P, dtype=np.float32)[::-1])
    put("ones", np.ones((P, P), np.float32))
    put("half_ones", (q // 64 == k // 64).astype(np.float32))
    put("mask_qk", np.where(k > q, NEG, 0).astype(np.float32))
    put("mask_kq", np.where(k <= q, NEG, 0).astype(np.float32))
    put("neg_suffix", np.where(q >= k, -1, 0).astype(np.float32))
    put("neg_ones", -np.ones((P, P), np.float32))
    strict = (q < k).astype(np.float32)
    incl = (q <= k).astype(np.float32)
    put("pair_masks", np.concatenate([strict, incl, strict, incl], 1))
    for level in range(LEVELS):
        b = 1 << level
        m = (q // (2 * b) == k // (2 * b)) & (q % (2 * b) < b) & (k % (2 * b) >= b)
        put(f"level{level}", -m.astype(np.float32))
    m = np.arange(384)
    rel = 255 - m
    ok = (rel >= 0) & (rel < 128)
    relf = np.maximum(rel, 1).astype(np.float32)
    large = 16 + (np.log(relf / np.float32(16)) / np.float32(math.log(8.0)) * np.float32(16)).astype(np.int32)
    large = np.minimum(large, 31)
    bucket = np.where(np.maximum(rel, 0) < 16, np.maximum(rel, 0), large)
    onehot = np.zeros((33, 384), np.float32)
    for j in m:
        if ok[j]:
            onehot[bucket[j], j] = 1
        else:
            onehot[32, j] = NEG
    put("buckets", onehot)
    freq = (np.float32(10000.0) ** (-np.arange(16, dtype=np.float32) / np.float32(16))).astype(np.float32)
    rot = np.zeros((P, 4), np.float32)
    for p in range(64, P):
        rot[p, 0] = freq[p % 16]
        rot[p, 1] = math.pi / 2 if p < 96 else 0
        rot[p, 2] = 0.25 if p < 96 else 0
        rot[p, 3] = -1 if 96 <= p < 112 else 1
    put("rotary", rot)
    return np.concatenate(cols, 1)


def alibi_rows():
    pos = np.arange(SEQ, dtype=np.float32)
    qa = np.stack([pos, np.ones(SEQ, np.float32)])
    ka = np.zeros((2, 4, SEQ), np.float32)
    for h in range(4):
        slope = 2.0 ** (-8.0 * (h + 1) / 4)
        ka[0, h] = -8 * slope
        ka[1, h] = 8 * slope * pos
    return np.concatenate([qa[:, None], ka], 1)


VECTORS = [("attn_norm", 16), ("ffn_norm", 16), ("final_norm", 8), ("ln_attn_pre_2", 8), ("ln_attn_post_2", 8),
           ("ln_ffn_pre_2", 8), ("ln_ffn_post_2", 8), ("mla_q_norm", 3), ("mla_kv_norm", 2), ("diff_subln_2", 1),
           ("mu_shift_2", 14), ("w_decay0_2", 4), ("w_iclr0_2", 4), ("k_k_2", 4), ("k_a_2", 4), ("r_k_2", 4),
           ("ln_x_w_2", 4), ("ln_x_b_2", 4), ("conv_w_2", 132), ("conv_b_2", 44)]

STAGES = ("even", "ffn0", "mla", "ffn1", "fnorm", "mix2", "ffn2")


def units_of(stages, d):
    units = []

    def rows(w, k0, kt, n0, n):
        return w[k0 * P:(k0 + kt) * P, n0:n0 + n].rearrange("(t p) n -> p t n", p=P)

    def linear(stage, w, total, width=256, kt=KT):
        for n0 in range(0, total, width):
            units.append((stage, rows(w, 0, kt, n0, min(width, total - n0))))

    def ffn(stage, gate, up, down):
        for n0 in range(0, HID, 256):
            units.append((stage + "_up", rows(gate, 0, KT, n0, 256)))
            units.append((stage + "_up", rows(up, 0, KT, n0, 256)))
        for k0 in range(0, HT, 2):
            units.append((stage + "_down", rows(down, k0, 2, 0, D)))

    for s in stages:
        if s == "even":
            w = d["even_w_in"][0]
            linear("even_qkv", w[:, 0:1536], 1536)
            for k0 in (0, 4):
                units.append(("even_qb", rows(w, k0, 4, 1536, 512)))
            units.append(("even_kvb", rows(w, 0, KT, 2048, 256)))
            linear("even_out", d["even_w_out"][0], D)
        if s in ("ffn0", "ffn1"):
            l = int(s[3])
            ffn(s, d["ffn_w_gate"][l], d["ffn_w_up"][l], d["ffn_w_down"][l])
        if s == "mla":
            w = d["mla_w_down"][0]
            linear("mla_down", w[:, 0:512], 512)
            units.append(("mla_down", rows(w, 0, KT, 512, 160)))
            for half in range(2):
                linear(f"mla_q{half}", d["mla_w_uq"][0][:, 768 * half:768 * (half + 1)], 768, 384, 3)
                units.append((f"mla_kv{half}", rows(d["mla_w_ukv"][0], 0, 2, 1024 * half, 1024)))
            linear("mla_out", d["mla_w_o"][0], D)
        if s == "mix2":
            w = d["w_in_2"][0]
            linear("diff_in", w[:, 1792:3328], 1536)
            linear("rwkv_in", w[:, 0:1792], 1792)
            linear("mix_out", d["w_out_2"][0], D)
        if s == "ffn2":
            ffn(s, d["w_up_2"][0][:, 0:HID], d["w_up_2"][0][:, HID:2 * HID], d["w_down_2"][0])
    first = {}
    for n, (name, _) in enumerate(units):
        first.setdefault(name, n)
    return units, first


NORMS = {"even": [("even", 8)], "ffn0": [("ffn0", 8)], "mla": [("mla", 8), ("q", 3), ("kv", 2)], "ffn1": [("ffn1", 8)],
         "fnorm": [("fnorm", 8)], "mix2": [("pre", 8), ("post", 8)], "ffn2": [("fpre", 8), ("fpost", 8)]}
LIN_TILES = {"even": 8 + 8 + 4 + 1 + 4 + 8, "mla": 6 + 2 * (8 + 4 + 4) + 8, "mix2": 8 + 8 + 14 + 8}


def build(nc, d, out, scratch, stages):
    units, first = units_of(stages, d)
    NU = len(units)
    norm_base, n_tiles, n_uses = {}, 0, 0
    for s in stages:
        for name, tiles in NORMS.get(s, []):
            norm_base[name] = (n_uses, n_tiles, tiles)
            n_uses += 1
            n_tiles += tiles
    lin_base, n_lin = {}, 0
    for s in stages:
        lin_base[s] = n_lin
        n_lin += LIN_TILES.get(s, 0)
    ffn_order = [s for s in stages if s.startswith("ffn")]
    hid_base = {s: HT * i for i, s in enumerate(ffn_order)}

    with ExitStack() as ctx:
        def sb(name, shape, dt=F32):
            return ctx.enter_context(nc.sbuf_tensor(name, shape, dt))

        def sem(name):
            return ctx.enter_context(nc.semaphore(name))

        bank = [ctx.enter_context(nc.psum_tensor(f"bank{i}", [P, 512], F32)) for i in range(8)]

        nconst = d["const_cols"].shape[1]
        con = sb("con", [P, nconst])
        X = sb("X", [P, KT, SEQ])
        XH = sb("XH", [P, KT, SEQ], F32R)
        XL = sb("XL", [P, KT, SEQ], F32R)
        w_raw = sb("w_raw", [P, 2, UW])
        w_hi = sb("w_hi", [P, 2, UW], F32R)
        w_lo = sb("w_lo", [P, 2, UW], F32R)
        identR = sb("identR", [P, P], F32R)
        masks = sb("masks", [P, 2, P], F32R)
        vec = sb("vec", [P, 3 * P])
        small = sb("small", [P, 160])
        ARENA = 96 * 256
        arena = sb("arena", [P, ARENA])

        def C(name):
            at, n = CONST_COLS[name]
            return con[:, at:at + n]

        ident = C("ident")
        taken = [0]

        def region(n, *shape):
            a = arena[:, taken[0]:taken[0] + n]
            taken[0] += n
            assert taken[0] <= ARENA, taken[0] * 4
            if len(shape) == 2:
                return a.rearrange("p (a b) -> p a b", b=shape[1])
            if len(shape) == 3:
                return a.rearrange("p (a b c) -> p a b c", b=shape[1], c=shape[2])
            if len(shape) == 4:
                return a.rearrange("p (a b c e) -> p a b c e", b=shape[1], c=shape[2], e=shape[3])
            return a

        vcol, vat = {}, 0
        for name, n in VECTORS:
            vcol[name] = vat
            vat += n

        def V(name, i):
            return vec[:, vcol[name] + i:vcol[name] + i + 1]

        w_loaded = [sem("w_loaded0"), sem("w_loaded1")]
        w_hi_ready = sem("w_hi_ready")
        w_lo_ready = sem("w_lo_ready")
        w_used = sem("w_used")
        setup_loaded = sem("setup_loaded")
        x_loaded = sem("x_loaded")
        consts_loaded = sem("consts_loaded")
        side_loaded = sem("side_loaded")
        turned = sem("turned")
        turned_out = sem("turned_out")
        setup_ready = sem("setup_ready")
        bias_row = sem("bias_row")
        bias_row_ready = sem("bias_row_ready")
        bias_out = sem("bias_out")
        bias_back = sem("bias_back")
        bias_turned = sem("bias_turned")
        winbias_ready = sem("winbias_ready")
        stored = sem("stored")
        act_link = sem("act_link")
        dve_link = sem("dve_link")
        pool_link = sem("pool_link")
        sq_ready = sem("sq_ready")
        sq_used = sem("sq_used")
        rstd_ready = sem("rstd_ready")
        normed = sem("normed")
        norm_hi = sem("norm_hi")
        norm_lo = [sem("norm_lo_even"), sem("norm_lo_odd")]
        normed_out = sem("normed_out")
        lin_ready = sem("lin_ready")
        lin_act = sem("lin_act")
        lin_free = sem("lin_free")
        g_ready = sem("g_ready")
        u_ready = sem("u_ready")
        silu_done = sem("silu_done")
        hid_done = sem("hid_done")
        hs_hi = sem("hs_hi")
        hs_lo = sem("hs_lo")
        down_ready = sem("down_ready")
        down_added = sem("down_added")
        cv_act = sem("cv_act")
        cv_one = sem("cv_one")
        cv_done = sem("cv_done")
        at_s = sem("at_s")
        at_m = sem("at_m")
        at_p = sem("at_p")
        at_t = sem("at_t")
        at_pt = sem("at_pt")
        at_o = sem("at_o")
        at_on = sem("at_on")
        ot_ready = sem("ot_ready")
        ot_turned = sem("ot_turned")
        ot_hi = sem("ot_hi")
        ot_lo = sem("ot_lo")
        sb_z = sem("sb_z")
        sb_ln = sem("sb_ln")
        sb_sp = sem("sb_sp")
        sb_sum = sem("sb_sum")
        sb_w = sem("sb_w")
        sb_o = sem("sb_o")
        sb_ohi = sem("sb_ohi")
        sb_olo = sem("sb_olo")
        pos_loaded = sem("pos_loaded")
        rope_arg = sem("rope_arg")
        rope_ready = sem("rope_ready")
        rope_done = sem("rope_done")
        alibi_loaded = sem("alibi_loaded")
        lam_loaded = sem("lam_loaded")
        lam_prod = sem("lam_prod")
        lam_exp = sem("lam_exp")
        sub_sum = sem("sub_sum")
        sub_rstd = sem("sub_rstd")
        krope_ready = sem("krope_ready")
        krope_spread = sem("krope_spread")
        wup_loaded = sem("wup_loaded")
        rw_lora = sem("rw_lora")
        rw_pre = sem("rw_pre")
        rw_sig = sem("rw_sig")
        rw_sqs = sem("rw_sqs")
        rw_sum = sem("rw_sum")
        rw_max = sem("rw_max")
        rw_rn = sem("rw_rn")
        rw_d = sem("rw_d")
        rw_bonus = sem("rw_bonus")
        rw_exp = sem("rw_exp")
        rw_vt = sem("rw_vt")
        rw_vtok = sem("rw_vtok")
        rw_facl = sem("rw_facl")
        rw_fac = sem("rw_fac")
        rw_bt = sem("rw_bt")
        rw_btc = sem("rw_btc")
        rw_a = sem("rw_a")
        rw_am = sem("rw_am")
        rw_xt0 = sem("rw_xt0")
        rw_x0 = sem("rw_x0")
        rw_x0c = sem("rw_x0c")
        rw_lvl = sem("rw_lvl")
        rw_t = sem("rw_t")
        rw_tc = sem("rw_tc")
        rw_xx = sem("rw_xx")
        rw_xn = sem("rw_xn")
        rw_p = sem("rw_p")
        rw_pc = sem("rw_pc")
        rw_u = sem("rw_u")
        rw_uc = sem("rw_uc")
        rw_y = sem("rw_y")
        rw_yc = sem("rw_yc")
        rw_s = sem("rw_s")
        rw_st = sem("rw_st")
        gn_mean = sem("gn_mean")
        gn_cent = sem("gn_cent")
        gn_var = sem("gn_var")
        gn_rstd = sem("gn_rstd")
        gn_gate = sem("gn_gate")
        gn_out = sem("gn_out")
        gn_hi = sem("gn_hi")
        gn_lo = sem("gn_lo")

        taken[0] = 0
        NS = region(1024, 2, 512)
        NTMP = region(1024, 2, 512)
        rstd = region(512)
        normed_ring = arena[:, 0:2048].rearrange("p (a b) -> p a b", b=512)

        def ring(k):
            return normed_ring[:, (2 + k) % 4, :]

        base0 = taken[0]
        taken[0] = base0
        xtok = region(4096, ST, D)
        vrow = region(3 * P, 3, P)
        taken[0] = base0
        Pb = region(3 * 512, 3, 512)
        PTb = region(2 * 512, 2, 512)
        base1 = taken[0]
        qTa = region(4 * SEQ, 4, SEQ)
        kTa = region(4 * SEQ, 4, SEQ)
        va = region(ST * 512, ST, 512)
        qTb = region(4 * SEQ, 4, SEQ)
        kTb = region(SEQ)
        vb = region(ST * P, ST, P)
        otok_e = region(ST * 512, ST, 512)
        winbias = region(8 * 256, 8, 256)
        Sb = region(2 * 512, 2, 512)
        SBL = region(3 * 1280, 3, 1280)
        taken[0] = base0
        hid = region(HT * SEQ, HT, SEQ)
        sg = region(2 * 512, 2, 512)
        cv = region(4 * 512, 4, 512)
        Y2 = region(KT * SEQ, KT, SEQ)
        taken[0] = base1
        qc = region(8 * SEQ, 8, SEQ)
        kc = region(8 * SEQ, 8, SEQ)
        vm = region(ST * 512, ST, 512)
        otok_m = region(ST * D, ST, D)
        cq = region(5 * SEQ, 5, SEQ)
        krope = region(SEQ)
        rotab = region(SEQ)
        rtmp = region(2 * SEQ, 2, SEQ)
        posb = region(SEQ)
        taken[0] = base1
        otok_d = region(ST * 512, ST, 512)
        base2 = taken[0]
        qd = region(8 * SEQ, 8, SEQ)
        kd = region(8 * SEQ, 8, SEQ)
        vd = region(ST * 512, ST, 512)
        lamv = region(512)
        odt = region(512, ST, P)
        taken[0] = base2
        rr = region(4 * SEQ, 4, SEQ)
        sgw = region(4 * SEQ, 4, SEQ)
        kk = region(4 * SEQ, 4, SEQ)
        vv = region(4 * SEQ, 4, SEQ)
        aa = region(4 * SEQ, 4, SEQ)
        KR = region(4 * NCH * 2 * CH, 4, NCH, 2 * CH)
        vtok = region(NCH * 512, NCH, 512)
        lora = region(2 * SEQ, 2, SEQ)
        wup = NTMP
        taken[0] = base0
        RT = region(5 * 512, 5, 512)
        AM = arena[:, base2:base2 + 4096].rearrange("p (h n) -> p h n", h=8)
        taken[0] = base0
        Xi = region(1024, 2, 512)
        XiT = region(1024, 2, 512)
        P0 = region(512)
        P1 = rstd
        taken[0] = base1
        Tl = region(1024, 2, 512)
        BK = region(1024, 2, 512)
        Al = NS
        STt = lora[:, 0, 0:256].rearrange("p (a b) -> p a b", b=64)

        sinks = small[:, 0:8]
        rowmax = small[:, 8:16].rearrange("p (a b) -> p a b", b=4)
        negm = small[:, 16:24].rearrange("p (a b) -> p a b", b=4)
        rsum = small[:, 24:32].rearrange("p (a b) -> p a b", b=4)
        rinv = small[:, 32:36]
        esink = small[:, 36:44].rearrange("p (a b) -> p a b", b=4)
        lam = small[:, 44:48]
        ssd = small[:, 138:154]
        mu1 = small[:, 56:70]
        ka1 = small[:, 70:74]
        cmid = small[:, 74:90].rearrange("p (a b) -> p a b", b=4)
        cend = small[:, 90:106].rearrange("p (a b) -> p a b", b=4)
        fac = small[:, 106:122].rearrange("p (a b) -> p a b", b=4)
        facl = small[:, 122:138].rearrange("p (a b) -> p a b", b=4)
        tabx = small[0:33, 48:56]
        epsb = small[:, 154:158]
        subg = small[:, 158:159]

        brow = Sb[:, 0, :]
        winrev = otok_e.rearrange("p a b -> p (a b)").rearrange("p (h n) -> p h n", n=256)

        def rwkv_tile(j):
            return (rr, kk, vv, lora)[j // 4][:, j % 4, :]

        c0 = vcol["conv_w_2"]

        def V3(i, c, tap, half):
            at = c0 + 44 * tap + 22 * half + c
            return vec[:, bass.ds(i * 2 + at, 1)]

        def VB(i, c, half):
            at = vcol["conv_b_2"] + 22 * half + c
            return vec[:, bass.ds(i * 2 + at, 1)]

        OT_TILES = {"even": 4, "mla": 8, "mix2": 4}
        OT_AT = {"even": 4, "mla": 0, "mix2": 4}
        split_base, low_base, n_split, n_low = {}, {}, 0, [0, 0]
        for s in stages:
            for name, tiles in NORMS.get(s, []):
                low_base[name] = tuple(n_low)
                if name not in ("fnorm", "post", "fpost"):
                    split_base[name] = n_split
                    n_split += tiles
                    n_low = [n_low[0] + (tiles + 1) // 2, n_low[1] + tiles // 2]

        def low_ready(name, k):
            return norm_lo[k % 2], low_base[name][k % 2] + k // 2 + 1

        def causal_groups():
            return [[(3, 0, 4, 0)], [(2, 0, 3, 0)], [(0, 0, 1, 0), (1, 0, 2, 128)]]

        ATT = {}
        ATT["win"] = dict(groups=[[(2, 1, 2, 0), (3, 2, 2, 256)], [(0, 0, 1, 128), (1, 0, 2, 256)]], heads=8, dv=64,
                          q=lambda h: qTb[64 * (h // 4):64 * (h // 4) + 64, h % 4, :],
                          k=lambda h: kTb[64 * (h // 4):64 * (h // 4) + 64, :],
                          v=lambda h, j: vb[:, j, 64 * (h // 4):64 * (h // 4) + 64], scale=1.0, mask=False)
        for half in range(2):
            ATT[f"mla{half}"] = dict(groups=causal_groups(), heads=8, dv=64,
                                     q=lambda h: qc[0:96, h, :], k=lambda h: kc[0:96, h, :],
                                     v=lambda h, j: vm[:, j, 64 * h:64 * h + 64], scale=96.0 ** -0.5, mask=True)
        ATT["diff"] = dict(groups=causal_groups(), heads=8, dv=128,
                           q=lambda h: qd[0:66, h, :], k=lambda h: kd[0:66, h, :],
                           v=lambda h, j: vd[:, j, 128 * (h // 2):128 * (h // 2) + 128], scale=0.125, mask=True)
        att_order = []
        for s in stages:
            att_order += {"even": ["win"], "mla": ["mla0", "mla1"], "mix2": ["diff"]}.get(s, [])
        gb = hb = 0
        for a in att_order:
            ATT[a]["g0"], ATT[a]["h0"] = gb, hb
            ATT[a]["list"] = [(h, i, tiles) for h in range(8) for i, tiles in enumerate(ATT[a]["groups"])]
            gb += len(ATT[a]["list"])
            hb += 8
        ot_base = {}
        n_ot = 0
        for s in stages:
            ot_base[s] = n_ot
            n_ot += {"even": 4, "mla": 8, "mix2": 4}.get(s, 0)

        def split_pieces(u, raw, part):
            stage, src = units[u]
            kt, n = src.shape[1], src.shape[2]
            s = raw[:, u % 2, 0:kt * n]
            if stage.startswith("mla_q"):
                s = s.rearrange("p (a c) -> p a c", c=96)
                t = part[:, u % 2, 0:kt * 512].rearrange("p (a c) -> p a c", c=128)
                return [(t[:, :, 0:96], s), (t[:, :, 96:112], s[:, :, 80:96]), (t[:, :, 112:128], s[:, :, 64:80])]
            if stage == "mla_down" and n == 160:
                s = s.rearrange("p (a c) -> p a c", c=160)
                t = part[:, u % 2, 0:kt * 192].rearrange("p (a c) -> p a c", c=192)
                return [(t[:, :, 0:160], s), (t[:, :, 160:176], s[:, :, 144:160]), (t[:, :, 176:192], s[:, :, 128:144])]
            if stage == "even_qb":
                s = s.rearrange("p (k a t c) -> p k a t c", a=2, t=4, c=64)
                t = part[:, u % 2, 0:kt * n].rearrange("p (k t a c) -> p k t a c", a=2, t=4, c=64)
                return [(t[:, :, :, a, :], s[:, :, a, :, :]) for a in range(2)]
            if stage.startswith("mla_kv"):
                s = s.rearrange("p (k h c) -> p k h c", h=8, c=128)
                t = part[:, u % 2, 0:kt * n].rearrange("p (k a h c) -> p k a h c", a=2, h=8, c=64)
                return [(t[:, :, a, :, :], s[:, :, :, 64 * a:64 * a + 64]) for a in range(2)]
            return [(part[:, u % 2, 0:kt * n], s)]

        def wv(u, n, kt):
            return [w[:, u % 2, 0:kt * n].rearrange("p (t n) -> p t n", n=n) for w in (w_hi, w_lo)]

        x_final, before, n_down, n_out = {}, (turned_out, 1), 0, 0
        out_base = {}
        for s in stages:
            x_final[s] = before
            if s in ("even", "mla"):
                before = (lin_free, lin_base[s] + LIN_TILES[s] - KT)
            elif s in ("ffn0", "ffn1"):
                before = (down_added, n_down)
            else:
                out_base[s] = n_out
                before = (normed_out, n_out)
                n_out += KT
            if s.startswith("ffn"):
                n_down += KT
        x_final["end"] = before
        down_base = {s: KT * i for i, s in enumerate(ffn_order)}

        def ffn_weights(s):
            if s == "ffn2":
                w = d["w_up_2"][0]
                return w[:, 0:HID], w[:, HID:2 * HID], d["w_down_2"][0]
            l = int(s[3])
            return d["ffn_w_gate"][l], d["ffn_w_up"][l], d["ffn_w_down"][l]

        def norm_plan(name):
            use, t0, tiles = norm_base[name]
            src, col, gain, done = {
                "even": (X, 0, ("attn_norm", 0), x_final.get("even")),
                "ffn0": (X, 0, ("ffn_norm", 0), x_final.get("ffn0")),
                "mla": (X, 0, ("attn_norm", 8), x_final.get("mla")),
                "q": (cq, 0, ("mla_q_norm", 0), (lin_free, lin_base.get("mla", 0))),
                "kv": (cq, 3, ("mla_kv_norm", 0), (lin_free, lin_base.get("mla", 0) + 3)),
                "ffn1": (X, 0, ("ffn_norm", 8), x_final.get("ffn1")),
                "fnorm": (X, 0, ("final_norm", 0), x_final.get("fnorm")),
                "pre": (X, 0, ("ln_attn_pre_2", 0), x_final.get("mix2")),
                "post": (Y2, 0, ("ln_attn_post_2", 0), (lin_free, lin_base.get("mix2", 0) + LIN_TILES["mix2"] - KT)),
                "fpre": (X, 0, ("ln_ffn_pre_2", 0), x_final.get("ffn2")),
                "fpost": (Y2, 0, ("ln_ffn_post_2", 0), (down_added, down_base.get("ffn2"))),
            }[name]
            return use, t0, tiles, src, col, gain, done

        XH_FREE = {"even": None, "ffn0": "ffn0_up", "mla": "mla_down", "q": "mla_q0", "kv": "mla_q0", "ffn1": "ffn1_up",
                   "pre": "diff_in", "fpre": "ffn2_up"}

        def tok_units(stage):
            return [u for u in range(NU) if units[u][0] == stage]

        def chunk(n):
            return slice(n * CH, (n + 1) * CH)

        def base_of(h):
            return 64 * (h % 2)

        def half_blocks(x, level, odd):
            b = 1 << level
            return x.rearrange("p (n e b) -> p n e b", e=2, b=b)[:, :, odd, :]

        GN = ((4, 5, 6), (0, 1, 7))

        SBOFF = {0: 0, 1: 512, 3: 896, 2: 1024}
        SBANK = {0: (0, 0), 1: (1, 0), 3: (1, 384), 2: (2, 0)}

        block = ctx.enter_context(nc.Block())

        @block.sync
        def _(sp):
            sp.dma_start(con[:, 0:P], d["const_cols"][:, 0:P]).then_inc(setup_loaded, 16)
            sp.dma_start(vrow[:, :, :], d["vec_rows"].rearrange("(a p) n -> p a n", p=P)).then_inc(setup_loaded, 16)
            sp.dma_start(xtok[:, :, :], d["x"][0].rearrange("(a p) n -> p a n", p=P)).then_inc(x_loaded, 16)
            sp.dma_start(con[:, P:nconst], d["const_cols"][:, P:nconst]).then_inc(consts_loaded, 16)

            def load(slot, src):
                kt, n = src.shape[1], src.shape[2]
                dst = w_raw[:, slot, 0:kt * n].rearrange("p (t n) -> p t n", n=n)
                sp.dma_start(dst, src).then_inc(w_loaded[slot], 16)

            def load_plain(u):
                if u >= 2:
                    sp.wait_ge(w_lo_ready, u - 1)
                load(u % 2, units[u][1])

            u = 0
            while u < NU:
                stage = units[u][0]
                if stage.endswith("_up"):
                    gate, up, _ = ffn_weights(stage[:4])
                    load_plain(u)
                    load_plain(u + 1)
                    with sp.Fori(1, HT // 2) as i:
                        for c, w in enumerate((gate, up)):
                            sp.wait_ge(w_lo_ready, i * 2 + (u + c - 1))
                            load((u + c) % 2, w[:, bass.ds(i * 256, 256)].rearrange("(t p) n -> p t n", p=P))
                    u += HT
                elif stage.startswith("ffn"):
                    down = ffn_weights(stage[:4])[2]
                    load_plain(u)
                    load_plain(u + 1)
                    with sp.Fori(1, 5) as i:
                        for c in range(2):
                            sp.wait_ge(w_lo_ready, i * 2 + (u + c - 1))
                            src = down[bass.ds(i * (4 * P) + c * 2 * P, 2 * P), :]
                            load((u + c) % 2, src.rearrange("(t p) n -> p t n", p=P))
                    load_plain(u + 10)
                    u += HT // 2
                else:
                    load_plain(u)
                    u += 1
            for s in range(ST):
                sp.wait_ge(turned_out, 9 + 2 * s + 2)
                sp.dma_start(out[0].rearrange("(a p) n -> a p n", p=P)[s], xtok[:, s, :]).then_inc(stored, 16)
            sp.wait_ge(stored, 16 * ST)

        @block.gpsimd
        def _(pool):
            links = [0]

            def link(ins):
                links[0] += 1
                ins.then_inc(pool_link, 1)
                pool.wait_ge(pool_link, links[0])

            def norm_split(name):
                use, t0, tiles, src, col, gain, done = norm_plan(name)
                for k in range(0, tiles, 2):
                    pool.wait_ge(norm_hi, split_base[name] + k + 1)
                    pool.tensor_tensor(XL[:, col + k, :], ring(k), XH[:, col + k, :].bitcast(F32),
                                       ALU.subtract).then_inc(norm_lo[0], 1)

            if "even" in stages:
                pool.dma_start(sinks, d["even_sinks"].broadcast_to([P, 8])).then_inc(side_loaded, 16)
                pool.dma_start(tabx[0:32, :], d["rel_bias_table"]).then_inc(side_loaded, 16)
                pool.wait_ge(bias_row_ready, 1)
                pool.dma_start(scratch, brow[0:8, 0:384]).then_inc(bias_out, 16)
                norm_split("even")
                pool.wait_ge(bias_out, 16)
                for h in range(8):
                    src = bass.AP(scratch.tensor, scratch.offset + 384 * h, [[1, P], [1, 256]])
                    pool.dma_start(winrev[:, h, :], src).then_inc(bias_back, 16)
            for s in stages:
                if s in ("ffn0", "ffn1"):
                    norm_split(s)
                if s == "ffn2":
                    norm_split("fpre")
                if s == "mla":
                    norm_split("mla")
                    pool.dma_start(posb.bitcast(I32), d["positions"].broadcast_to([P, SEQ])).then_inc(pos_loaded, 16)
                    norm_split("q")
                    norm_split("kv")
                    pool.wait_ge(norm_lo[0], low_base["kv"][0] + 1)
                    for half in range(2):
                        for h in range(8):
                            if half or h:
                                pool.wait_ge(rope_done, 8 * half + h)
                            pool.wait_ge(lin_free, lin_base[s] + 6 + 16 * half + h + 1)
                            pool.tensor_tensor(qc[64:96, h, :], qc[64:96, h, :], rtmp[64:96, h % 2, :],
                                               ALU.add).then_inc(rope_done, 1)
                if s == "mix2":
                    norm_split("pre")
                    pool.dma_start(lamv[:, 0:256], d["lambdas"].broadcast_to([P, 256])).then_inc(lam_loaded, 16)
                    for h in range(8):
                        pool.dma_start(qd[64:66, h, :], d["alibi"][:, 0, :]).then_inc(alibi_loaded, 16)
                        pool.dma_start(kd[64:66, h, :], d["alibi"][:, 1 + h // 2, :]).then_inc(alibi_loaded, 16)
                    for parity in range(2):
                        pool.wait_ge(*low_ready("pre", KT - 2 + parity))
                    pool.dma_start(wup[0:64, 0, :], d["w_decay_up_2"][0]).then_inc(wup_loaded, 16)
                    pool.dma_start(wup[64:128, 0, :], d["w_iclr_up_2"][0]).then_inc(wup_loaded, 16)
                    pool.dma_start(wup[:, 1, :], d["w_gate_up_2"][0]).then_inc(wup_loaded, 16)
                    for n in range(NCH):
                        for level in range(1, LEVELS):
                            for g in range(2):
                                at = (n * (LEVELS - 1) + level - 1) * 2 + g
                                if level == 1 and g == 0:
                                    pool.wait_ge(rw_am, 8 * n + 8)
                                if at >= 2:
                                    pool.wait_ge(rw_t, at - 1)
                                lv = C(f"level{level}").unsqueeze(1).broadcast_to([P, 4, P])
                                pool.tensor_tensor(Al[:, g, :].rearrange("p (h n) -> p h n", n=P),
                                                   AM[:, 4 * g:4 * g + 4, 0:128], lv, ALU.mult).then_inc(rw_lvl, 1)

        @block.scalar
        def _(act):
            links = [0]

            def link(ins):
                links[0] += 1
                ins.then_inc(act_link, 1)
                act.wait_ge(act_link, links[0])

            def exp_and_log():
                act.preload_act_table_set("natural_log_exp_and_others")

            def split(u):
                if u >= NU:
                    return
                act.wait_ge(w_loaded[u % 2], 16 * (u // 2 + 1))
                if u >= 2:
                    act.wait_ge(w_used, u - 1)
                for to, frm in split_pieces(u, w_raw, w_hi):
                    last = act.activation(to, frm, ACT.Copy)
                last.then_inc(w_hi_ready, 1)

            def root_mean_squares(name):
                use, t0, tiles, src, col, gain, done = norm_plan(name)
                for parity in range(2):
                    if low_base[name][parity]:
                        act.wait_ge(norm_lo[parity], low_base[name][parity])
                for k in range(tiles):
                    act.wait_ge(done[0], done[1] + k + 1)
                    if t0 + k >= 2:
                        act.wait_ge(sq_used, t0 + k - 1 if k >= 2 else t0)
                    act.activation(NS[:, k % 2, :], src[:, col + k, :], ACT.Square,
                                   scale=(tiles * P) ** -0.5).then_inc(sq_ready, 1)
                act.wait_ge(sq_used, t0 + tiles)
                link(act.activation(rstd, bank[7][:, :], ACT.Ln, bias=epsb[:, 0:1]))
                act.activation(rstd, rstd, ACT.Exp, scale=-0.5).then_inc(rstd_ready, 1)

            def norm(name):
                use, t0, tiles, src, col, gain, done = norm_plan(name)
                root_mean_squares(name)
                if name in XH_FREE:
                    for k in range(tiles):
                        act.wait_ge(normed, split_base[name] + k + 1)
                        if k == 0 and XH_FREE[name] and first[XH_FREE[name]] > 0:
                            act.wait_ge(w_used, first[XH_FREE[name]])
                        act.activation(XH[:, col + k, :], ring(k), ACT.Copy).then_inc(norm_hi, 1)

            def head_pairs_out(s, gain):
                for t in range(OT_TILES[s]):
                    act.wait_ge(ot_turned, ot_base[s] + t + 1)
                    dst = XH[:, OT_AT[s] + t, :]
                    if gain is None:
                        act.activation(dst, bank[t % 2][:, :], ACT.Copy).then_inc(ot_hi, 1)
                    else:
                        act.activation(dst, bank[t % 2][:, :], ACT.Copy, scale=gain).then_inc(ot_hi, 1)

            def attention(name):
                A = ATT[name]
                groups, g0, h0 = A["list"], A["g0"], A["h0"]

                def evacuate(n):
                    g = g0 + n
                    h, gi, tiles = groups[n]
                    lo, hi = tiles[0][3], tiles[-1][3] + P * tiles[-1][2]
                    act.wait_ge(at_t, g + 1)
                    if g >= 2:
                        act.wait_ge(at_o, g - 1)
                    act.activation(PTb[:, g % 2, lo:hi], bank[3 + g % 2][:, lo:hi], ACT.Copy).then_inc(at_pt, 1)

                for n, (h, gi, tiles) in enumerate(groups):
                    g, hh = g0 + n, h0 + h
                    act.wait_ge(at_m, g + 1)
                    if g >= 3:
                        act.wait_ge(at_t, g - 2)
                    if gi == 0 and hh >= 2:
                        act.wait_ge(at_on, hh - 1)
                    src = bank[g % 3] if name != "win" else Sb[:, g % 2, :]
                    if name == "win" and gi == len(A["groups"]) - 1:
                        act.activation(esink[:, hh % 2, :], negm[:, hh % 2, :], ACT.Exp, bias=sinks[:, h:h + 1])
                    for i, k0, nk, c in tiles:
                        last = act.activation(Pb[:, g % 3, c:c + P * nk], src[:, c:c + P * nk], ACT.Exp,
                                              bias=negm[:, hh % 2, i:i + 1], scale=A["scale"],
                                              accum_out=rsum[:, hh % 2, i:i + 1])
                    last.then_inc(at_p, 1)
                    if n >= 1:
                        evacuate(n - 1)
                evacuate(len(groups) - 1)

            def stick_breaking():
                def ln_part(h):
                    act.wait_ge(sb_z, h + 1)
                    if h >= 3:
                        act.wait_ge(sb_o, h - 2)
                    for b, (lo, n) in enumerate(((0, 512), (512, 512), (1024, 256))):
                        last = act.activation(SBL[:, h % 3, lo:lo + n], bank[3 * (h % 2) + b][:, 0:n], ACT.Abs)
                    link(last)
                    link(act.activation(SBL[:, h % 3, :], SBL[:, h % 3, :], ACT.Exp, scale=-1.0))
                    act.activation(SBL[:, h % 3, :], SBL[:, h % 3, :], ACT.Ln, bias=1.0).then_inc(sb_ln, 1)

                def weights(h):
                    act.wait_ge(sb_sum, h + 1)
                    for b, (lo, n) in enumerate(((0, 512), (512, 512), (1024, 256))):
                        last = act.activation(SBL[:, h % 3, lo:lo + n], bank[3 * (h % 2) + b][:, 0:n], ACT.Exp)
                    last.then_inc(sb_w, 1)

                ln_part(0)
                ln_part(1)
                for h in range(8):
                    weights(h)
                    if h % 2 == 0 and h >= 2:
                        out_pair(h // 2 - 1)
                    if h + 2 < 8:
                        ln_part(h + 2)
                out_pair(3)

            def out_pair(t):
                act.wait_ge(sb_o, 2 * t + 2)
                if t == 0:
                    act.wait_ge(w_used, first["even_out"])
                act.activation(XH[:, t, :], bank[6 + t % 2][:, :], ACT.Copy).then_inc(sb_ohi, 1)

            def even():
                norm("even")
                for u in tok_units("even_qkv") + tok_units("even_qb") + tok_units("even_kvb"):
                    split(u + 1)
                stick_breaking()
                attention("win")
                head_pairs_out("even", None)
                for u in tok_units("even_out"):
                    split(u + 1)

            def ffn_hidden_split(s, u0, j):
                for c in range(2):
                    k = 2 * j + c
                    act.activation(XH[:, k % 4, :], hid[:, k, :], ACT.Copy).then_inc(hs_hi, 1)

            def ffn(s):
                norm(s if s != "ffn2" else "fpre")
                u0, h0 = first[s + "_up"], hid_base[s]
                def body(i):
                    act.wait_ge(w_loaded[(u0 + 1) % 2], i * 16 + 16 * ((u0 + 1) // 2 + 1))
                    act.wait_ge(w_used, i * 2 + u0)
                    act.activation(w_hi[:, (u0 + 1) % 2, :], w_raw[:, (u0 + 1) % 2, :], ACT.Copy).then_inc(w_hi_ready, 1)
                    for c in range(2):
                        act.wait_ge(g_ready, i * 2 + (h0 + c + 1))
                        if not (isinstance(i, int) and h0 == 0):
                            act.wait_ge(hid_done, i * 2 + h0)
                        if s != "ffn2":
                            act.activation(sg[:, c, :], bank[c][:, :], ACT.Silu).then_inc(silu_done, 1)
                        else:
                            act.activation(cv[:, c, :], bank[c][:, :], ACT.Identity, scale=V3(i, c, 2, 0),
                                           bias=VB(i, c, 0)).then_inc(cv_act, 1)
                    act.wait_ge(w_loaded[u0 % 2], i * 16 + 16 * (u0 // 2 + 2))
                    act.wait_ge(w_used, i * 2 + (u0 + 1))
                    act.activation(w_hi[:, u0 % 2, :], w_raw[:, u0 % 2, :], ACT.Copy).then_inc(w_hi_ready, 1)
                    if s == "ffn2":
                        for c in range(2):
                            act.wait_ge(u_ready, i * 2 + (h0 + c + 1))
                            act.activation(cv[:, 2 + c, :], bank[2 + c][:, :], ACT.Identity, scale=V3(i, c, 2, 1),
                                           bias=VB(i, c, 1)).then_inc(cv_act, 1)
                        for c in range(2):
                            act.wait_ge(cv_done, i * 4 + (c + 1))
                            act.activation(sg[:, c, :], cv[:, c, :], ACT.Gelu_apprx_tanh).then_inc(silu_done, 1)
                body(0)
                with act.Fori(1, HT // 2) as i:
                    body(i)
                exp_and_log()
                u0 = first[s + "_down"]
                act.wait_ge(hid_done, h0 + 2)
                act.wait_ge(w_used, u0)
                ffn_hidden_split(s, u0, 0)
                split(u0 + 1)
                act.wait_ge(hid_done, h0 + HT)
                ffn_hidden_split(s, u0, 1)
                with act.Fori(0, 4) as i:
                    for c in range(2):
                        slot = (u0 + c) % 2
                        act.wait_ge(w_loaded[slot], i * 16 + 16 * ((u0 + 2 + c) // 2 + 1))
                        act.wait_ge(w_used, i * 2 + (u0 + 1 + c))
                        act.activation(w_hi[:, slot, :], w_raw[:, slot, :], ACT.Copy).then_inc(w_hi_ready, 1)
                        for e in range(2):
                            act.activation(XH[:, 2 * c + e:2 * c + e + 1, :],
                                           hid[:, bass.ds(i * 4 + (4 + 2 * c + e), 1), :], ACT.Copy).then_inc(hs_hi, 1)
                split(u0 + 10)
                ffn_hidden_split(s, u0, 10)
                split(u0 + 11)
                if s == "ffn2":
                    norm("fpost")

            def mla():
                norm("mla")
                act.wait_ge(rope_arg, 1)
                act.activation(rotab[64:128, :], rotab[64:128, :], ACT.Sin).then_inc(rope_ready, 1)
                exp_and_log()
                for u in tok_units("mla_down"):
                    split(u + 1)
                norm("q")
                norm("kv")
                L = lin_base["mla"] + 6
                for half in range(2):
                    if half == 0:
                        act.wait_ge(krope_ready, 1)
                        act.activation(kc[64:96, :, :], krope[64:96, :].unsqueeze(1).broadcast_to([32, 8, SEQ]),
                                       ACT.Copy).then_inc(krope_spread, 1)
                    for u in tok_units(f"mla_q{half}"):
                        split(u + 1)
                        for t in range(4):
                            h = 4 * (u - first[f"mla_q{half}"]) + t
                            act.wait_ge(lin_ready, L + h + 1)
                            act.activation(qc[0:64, h, :], bank[(L + h) % 4][0:64, :], ACT.Copy).then_inc(lin_act, 1)
                    L += 8
                    for u in tok_units(f"mla_kv{half}"):
                        split(u + 1)
                        for t in range(4):
                            act.wait_ge(lin_ready, L + t + 1)
                            act.activation(kc[0:64, 2 * t, :], bank[(L + t) % 4][0:64, :], ACT.Copy).then_inc(lin_act, 1)
                    L += 8
                    attention(f"mla{half}")
                head_pairs_out("mla", None)
                for u in tok_units("mla_out"):
                    split(u + 1)

            def mix2():
                norm("pre")
                L = lin_base["mix2"]
                act.wait_ge(lam_prod, 1)
                act.activation(lam[:, 0:2], lam[:, 0:2], ACT.Exp).then_inc(lam_exp, 1)
                for u in tok_units("diff_in"):
                    split(u + 1)
                    j = u - first["diff_in"]
                    if j < 4:
                        for t in range(2):
                            h = 2 * (j % 2) + t
                            act.wait_ge(lin_ready, L + 2 * j + t + 1)
                            act.activation((qd, kd)[j // 2][0:64, 2 * h, :], bank[(L + 2 * j + t) % 4][0:64, :],
                                           ACT.Copy).then_inc(lin_act, 1)
                attention("diff")
                act.wait_ge(sub_sum, 1)
                link(act.activation(ssd, ssd, ACT.Ln, scale=1.0 / 128, bias=epsb[:, 1:2]))
                act.activation(ssd, ssd, ACT.Exp, scale=-0.5).then_inc(sub_rstd, 1)
                L += 16
                act.wait_ge(at_on, ATT["diff"]["h0"] + 8)
                for u in tok_units("rwkv_in"):
                    split(u + 1)
                    for t in range(2):
                        j = 2 * (u - first["rwkv_in"]) + t
                        act.wait_ge(lin_ready, L + j + 1)
                        act.activation(rwkv_tile(j), bank[(L + j) % 4][:, :], ACT.Identity,
                                       scale=mu1[:, j:j + 1]).then_inc(lin_act, 1)
                act.wait_ge(w_used, first["mix_out"])
                head_pairs_out("mix2", subg)
                act.wait_ge(lin_free, L + 14)
                act.activation(lora[0:64, 0, :], lora[0:64, 0, :], ACT.Tanh)
                act.activation(lora[:, 1, :], lora[:, 1, :], ACT.Sigmoid).then_inc(rw_lora, 1)
                for t in range(4):
                    act.wait_ge(rw_pre, 2 * t + 1)
                    act.activation(sgw[:, t, :], bank[2 + (2 * t) % 4][:, :], ACT.Sigmoid,
                                   bias=V("w_decay0_2", t)).then_inc(rw_sig, 1)
                    act.wait_ge(rw_pre, 2 * t + 2)
                    act.activation(aa[:, t, :], bank[2 + (2 * t + 1) % 4][:, :], ACT.Sigmoid,
                                   bias=V("w_iclr0_2", t)).then_inc(rw_sig, 1)
                exp_and_log()
                for t in range(4):
                    act.wait_ge(rw_d, t + 1)
                    act.wait_ge(rw_sum, 2 * t + 2)
                    act.activation(RT[:, 2, :], RT[:, 4, :], ACT.Exp, scale=DS)
                    act.activation(RT[:, 4, :], RT[:, 4, :], ACT.Exp, scale=-DS)
                    act.activation(RT[:, 3, :], RT[:, 3, :], ACT.Exp, scale=-DS).then_inc(rw_exp, 1)
                    act.wait_ge(rw_max, t + 1)
                    link(act.activation(RT[:, 1, :], RT[:, 1, :], ACT.Ln, scale=2.0 ** 30))
                    act.activation(RT[:, 1, :], RT[:, 1, :], ACT.Exp, scale=-0.5, bias=epsb[:, 2:3]).then_inc(rw_rn, 1)
                    act.wait_ge(rw_vt, t + 1)
                    act.activation(vtok[:, :, t * P:(t + 1) * P], bank[6][:, :].rearrange("p (a b) -> p a b", b=P),
                                   ACT.Copy).then_inc(rw_vtok, 1)
                act.wait_ge(rw_facl, 1)
                act.activation(fac[:, :, 0:3], facl[:, :, 0:3], ACT.Exp, scale=-DS).then_inc(rw_fac, 1)
                for n in range(NCH):
                    for part in range(2):
                        act.wait_ge(rw_bt, 2 * n + part + 1)
                        if n >= 1:
                            act.wait_ge(rw_s, n)
                        act.activation(BK[:, part, :], bank[6 + part][:, :], ACT.Copy).then_inc(rw_btc, 1)
                    for g in range(2):
                        act.wait_ge(rw_x0, 2 * n + g + 1)
                        act.activation(Xi[:, g, :], bank[4 + g][:, :], ACT.Copy).then_inc(rw_x0c, 1)
                    for level in range(1, LEVELS):
                        for g in range(2):
                            at = (n * (LEVELS - 1) + level - 1) * 2 + g
                            act.wait_ge(rw_t, at + 1)
                            if at >= 2:
                                act.wait_ge(rw_xx, at - 1)
                            act.activation(Tl[:, g, :], bank[g][:, :], ACT.Copy).then_inc(rw_tc, 1)
                    act.wait_ge(rw_p, n + 1)
                    for e in range(2):
                        last = act.activation(P0.rearrange("p (t e v) -> p t e v", e=2, v=64)[:, :, e, :],
                                              bank[e][:, 0:256].rearrange("p (t v) -> p t v", v=64), ACT.Copy, scale=-1.0)
                    last.then_inc(rw_pc, 1)
                    act.wait_ge(rw_u, n + 1)
                    act.activation(P1, bank[4][:, :], ACT.Copy).then_inc(rw_uc, 1)
                def group_rstd(t):
                    act.wait_ge(gn_var, t + 1)
                    link(act.activation(XiT[:, t % 2, :], bank[GN[t % 2][1]][:, :], ACT.Ln, scale=1.0 / 64,
                                        bias=epsb[:, 3:4]))
                    act.activation(XiT[:, t % 2, :], XiT[:, t % 2, :], ACT.Exp, scale=-0.5).then_inc(gn_rstd, 1)

                group_rstd(0)
                for t in range(4):
                    if t < 3:
                        group_rstd(t + 1)
                    act.wait_ge(gn_out, t + 1)
                    act.activation(XH[:, t, :], Xi[:, t % 2, :], ACT.Copy).then_inc(gn_hi, 1)
                for u in tok_units("mix_out"):
                    split(u + 1)
                norm("post")

            exp_and_log()
            split(0)
            act.wait_ge(setup_ready, 1)
            act.wait_ge(turned_out, 1)
            if "even" in stages:
                act.wait_ge(side_loaded, 32)
            for s in stages:
                {"even": even, "mla": mla, "mix2": mix2, "fnorm": lambda: norm("fnorm")}.get(s, lambda: ffn(s))()

        @block.vector
        def _(dve):
            links = [0]

            def link(ins):
                links[0] += 1
                ins.then_inc(dve_link, 1)
                dve.wait_ge(dve_link, links[0])

            def split(u):
                if u >= NU:
                    return
                dve.wait_ge(w_hi_ready, u + 1)
                for (to, frm), (hi, _) in zip(split_pieces(u, w_raw, w_lo), split_pieces(u, w_raw, w_hi)):
                    last = dve.tensor_tensor(to, frm, hi.bitcast(F32), ALU.subtract)
                last.then_inc(w_lo_ready, 1)

            def norm(name):
                use, t0, tiles, src, col, (gname, gat), done = norm_plan(name)
                dve.wait_ge(rstd_ready, use + 1)
                for k in range(tiles):
                    if name in XH_FREE:
                        if k == 0 and low_base[name][0]:
                            dve.wait_ge(norm_lo[0], low_base[name][0])
                        if k >= 4:
                            dve.wait_ge(*low_ready(name, k - 4))
                        dve.scalar_tensor_tensor(ring(k), src[:, col + k, :], V(gname, gat + k), rstd,
                                                 ALU.mult, ALU.mult).then_inc(normed, 1)
                        for j in (k - 1, k):
                            if j > 0 and j % 2 and (j == k - 1 or j == tiles - 1):
                                dve.wait_ge(norm_hi, split_base[name] + j + 1)
                                dve.tensor_tensor(XL[:, col + j, :], ring(j), XH[:, col + j, :].bitcast(F32),
                                                  ALU.subtract).then_inc(norm_lo[1], 1)
                    elif name == "fnorm":
                        dve.scalar_tensor_tensor(X[:, k, :], X[:, k, :], V(gname, gat + k), rstd,
                                                 ALU.mult, ALU.mult).then_inc(normed_out, 1)
                    else:
                        links[0] += 1
                        dve.scalar_tensor_tensor(src[:, k, :], src[:, k, :], V(gname, gat + k), rstd,
                                                 ALU.mult, ALU.mult).then_inc(dve_link, 1)
                        for j in ((k - 1,) if k < tiles - 1 else (k - 1, k)):
                            if j >= 0:
                                dve.wait_ge(dve_link, links[0] - (k - j))
                                dve.tensor_tensor(X[:, j, :], X[:, j, :], src[:, j, :], ALU.add).then_inc(normed_out, 1)

            def head_pairs_out(s, gain):
                for t in range(OT_TILES[s]):
                    dve.wait_ge(ot_hi, ot_base[s] + t + 1)
                    dst = XL[:, OT_AT[s] + t, :]
                    hi = XH[:, OT_AT[s] + t, :].bitcast(F32)
                    dve.scalar_tensor_tensor(dst, bank[t % 2][:, :], 1.0 if gain is None else gain, hi,
                                             ALU.mult, ALU.subtract).then_inc(ot_lo, 1)

            def attention(name):
                A = ATT[name]
                groups, g0, h0 = A["list"], A["g0"], A["h0"]
                last_gi = len(A["groups"]) - 1

                def maxima(n):
                    g = g0 + n
                    h, gi, tiles = groups[n]
                    hh = h0 + h
                    i0, i1 = min(t[0] for t in tiles), max(t[0] for t in tiles)
                    src = bank[g % 3]
                    dve.wait_ge(at_s, g + 1)
                    if name == "win":
                        if g >= 2:
                            dve.wait_ge(at_p, g - 1)
                        for i, k0, nk, c in tiles:
                            last = dve.scalar_tensor_tensor(Sb[:, g % 2, c:c + P * nk], src[:, c:c + P * nk], 0.125,
                                                            winbias[:, h, 256 - P * nk:256], ALU.mult, ALU.add)
                        link(last)
                        src = Sb[:, g % 2, :]
                    if gi == 0 and hh >= 2:
                        dve.wait_ge(at_p, g0 + (h - 1) * (last_gi + 1) if h >= 2 else g0)
                    for i, k0, nk, c in tiles:
                        last = dve.tensor_reduce(rowmax[:, hh % 2, i:i + 1], src[:, c:c + P * nk], AX.X, ALU.max)
                    link(last)
                    if name == "win":
                        dve.tensor_scalar(negm[:, hh % 2, i0:i1 + 1], rowmax[:, hh % 2, i0:i1 + 1], sinks[:, h:h + 1],
                                          -1.0, ALU.max, ALU.mult).then_inc(at_m, 1)
                    else:
                        dve.tensor_scalar(negm[:, hh % 2, i0:i1 + 1], rowmax[:, hh % 2, i0:i1 + 1], -A["scale"], None,
                                          ALU.mult).then_inc(at_m, 1)

                def head_end(h):
                    hh = h0 + h
                    dv = A["dv"]
                    dve.wait_ge(at_o, g0 + (h + 1) * (last_gi + 1))
                    if name == "win":
                        link(dve.tensor_tensor(rsum[:, hh % 2, :], rsum[:, hh % 2, :], esink[:, hh % 2, :], ALU.add))
                    link(dve.reciprocal(rinv, rsum[:, hh % 2, :]))
                    if name == "diff" and h % 2:
                        link(dve.tensor_scalar(rinv, rinv, lam[:, 2:3], None, ALU.mult))
                    o = bank[5 + hh % 2][:, 0:4 * dv].rearrange("p (i v) -> p i v", v=dv)
                    r = rinv.unsqueeze(2).broadcast_to([P, 4, dv])
                    if name == "win":
                        dst = otok_e[:, :, 64 * h:64 * h + 64]
                    elif name == "diff":
                        dst = otok_d[:, :, 128 * (h // 2):128 * (h // 2) + 128]
                        if h % 2:
                            dst = odt
                    else:
                        n = 8 * int(name[3]) + h
                        dst = otok_m[:, :, 64 * n:64 * n + 64]
                    dve.tensor_tensor(dst, o, r, ALU.mult).then_inc(at_on, 1)
                    if name == "diff" and h % 2:
                        dve.wait_ge(at_on, hh + 1)
                        full = otok_d[:, :, 128 * (h // 2):128 * (h // 2) + 128]
                        link(dve.tensor_tensor(full, full, odt, ALU.subtract))
                        link(dve.tensor_tensor(odt, full, full, ALU.mult))
                        last = dve.tensor_reduce(ssd[:, 4 * (h // 2):4 * (h // 2) + 4], odt, AX.X, ALU.add)
                        if h == 7:
                            last.then_inc(sub_sum, 1)
                        else:
                            link(last)

                for n, (h, gi, tiles) in enumerate(groups):
                    maxima(n)
                    if gi == 1 and h >= 1:
                        head_end(h - 1)
                head_end(7)

            def stick_breaking():
                def softplus(h):
                    dve.wait_ge(sb_ln, h + 1)
                    for b, (lo, n) in enumerate(((0, 512), (512, 512), (1024, 256))):
                        last = dve.scalar_tensor_tensor(SBL[:, h % 3, lo:lo + n], bank[3 * (h % 2) + b][:, 0:n], 0.0,
                                                        SBL[:, h % 3, lo:lo + n], ALU.max, ALU.add)
                    last.then_inc(sb_sp, 1)

                def out_pair(t):
                    dve.wait_ge(sb_ohi, t + 1)
                    dve.tensor_tensor(XL[:, t, :], bank[6 + t % 2][:, :], XH[:, t, :].bitcast(F32),
                                      ALU.subtract).then_inc(sb_olo, 1)

                softplus(0)
                for h in range(1, 8):
                    softplus(h)
                    if h % 2 == 0 and h >= 4:
                        out_pair(h // 2 - 2)
                out_pair(2)
                out_pair(3)

            def even():
                norm("even")
                L = lin_base["even"]
                for u in tok_units("even_qkv"):
                    split(u + 1)
                    j = u - first["even_qkv"]
                    for t in range(2 if j < 4 else 4):
                        dve.wait_ge(lin_ready, L + 1)
                        b = bank[L % 4]
                        if j < 2:
                            dve.tensor_scalar(qTa[:, 2 * j + t, :], b[:, :], 0.125, None, ALU.mult).then_inc(lin_free, 1)
                        elif j < 4:
                            dve.tensor_copy(kTa[:, 2 * (j - 2) + t, :], b[:, :]).then_inc(lin_free, 1)
                        else:
                            dve.tensor_copy(va[:, t, 256 * (j - 4):256 * (j - 3)], b[:, 0:256]).then_inc(lin_free, 1)
                        L += 1
                qb = tok_units("even_qb")
                split(qb[0] + 1)
                split(qb[1] + 1)
                for t in range(4):
                    dve.wait_ge(lin_ready, L + 1)
                    dve.tensor_copy(qTb[:, t, :], bank[L % 4][:, :]).then_inc(lin_free, 1)
                    L += 1
                split(qb[1] + 2)
                dve.wait_ge(lin_ready, L + 1)
                dve.tensor_copy(kTb, bank[L % 4][:, :]).then_inc(lin_free, 1)
                L += 1
                for t in range(4):
                    dve.wait_ge(lin_ready, L + 1)
                    dve.tensor_copy(vb[:, t, :], bank[L % 4][:, 0:P]).then_inc(lin_free, 1)
                    L += 1
                for j in range(4):
                    dve.wait_ge(bias_turned, j + 2)
                    dve.tensor_copy(winbias[:, 2 * j:2 * j + 2, :],
                                    bank[3 + j][:, :].rearrange("p (a b) -> p a b", b=256)).then_inc(winbias_ready, 1)
                stick_breaking()
                attention("win")
                head_pairs_out("even", None)
                residual("even_out", L)

            def residual(stage, L):
                for u in tok_units(stage):
                    split(u + 1)
                    for t in range(2):
                        n = 2 * (u - first[stage]) + t
                        dve.wait_ge(lin_ready, L + n + 1)
                        dve.tensor_tensor(X[:, n, :], X[:, n, :], bank[(L + n) % 4][:, :], ALU.add).then_inc(lin_free, 1)

            def hidden_split(j):
                for c in range(2):
                    k = 2 * j + c
                    dve.wait_ge(hs_hi, hs_count[0] + 1)
                    dve.tensor_tensor(XL[:, k % 4, :], hid[:, k, :], XH[:, k % 4, :].bitcast(F32),
                                      ALU.subtract).then_inc(hs_lo, 1)
                    hs_count[0] += 1

            hs_count = [0]

            def ffn(s):
                norm(s if s != "ffn2" else "fpre")
                u0, h0 = first[s + "_up"], hid_base[s]
                def body(i):
                    dve.wait_ge(w_hi_ready, i * 2 + (u0 + 2))
                    a = (u0 + 1) % 2
                    dve.tensor_tensor(w_lo[:, a, :], w_raw[:, a, :], w_hi[:, a, :].bitcast(F32),
                                      ALU.subtract).then_inc(w_lo_ready, 1)
                    if s == "ffn2":
                        for c in range(2):
                            taps(i, c, 0, c)
                    dve.wait_ge(w_hi_ready, i * 2 + (u0 + 3))
                    a = u0 % 2
                    dve.tensor_tensor(w_lo[:, a, :], w_raw[:, a, :], w_hi[:, a, :].bitcast(F32),
                                      ALU.subtract).then_inc(w_lo_ready, 1)
                    if s == "ffn2":
                        for c in range(2):
                            taps(i, c, 1, 2 + c)
                    for c in range(2):
                        dve.wait_ge(silu_done, i * 2 + (h0 + c + 1))
                        if s != "ffn2":
                            dve.wait_ge(u_ready, i * 2 + (h0 + c + 1))
                            other = bank[2 + c][:, :]
                        else:
                            dve.wait_ge(cv_done, i * 4 + (3 + c))
                            other = cv[:, 2 + c, :]
                        dve.tensor_tensor(hid[:, bass.ds(i * 2 + c, 1), :], sg[:, c, :].unsqueeze(1),
                                          other.unsqueeze(1), ALU.mult).then_inc(hid_done, 1)
                body(0)
                with dve.Fori(1, HT // 2) as i:
                    body(i)
                u0 = first[s + "_down"]
                hidden_split(0)
                split(u0 + 1)
                hidden_split(1)
                hs0 = hs_count[0]
                with dve.Fori(0, 4) as i:
                    for c in range(2):
                        slot = (u0 + c) % 2
                        dve.wait_ge(w_hi_ready, i * 2 + (u0 + 3 + c))
                        dve.tensor_tensor(w_lo[:, slot, :], w_raw[:, slot, :], w_hi[:, slot, :].bitcast(F32),
                                          ALU.subtract).then_inc(w_lo_ready, 1)
                        for e in range(2):
                            j = 2 * c + e
                            dve.wait_ge(hs_hi, i * 4 + (hs0 + j + 1))
                            dve.tensor_tensor(XL[:, j:j + 1, :], hid[:, bass.ds(i * 4 + (4 + j), 1), :],
                                              XH[:, j:j + 1, :].bitcast(F32), ALU.subtract).then_inc(hs_lo, 1)
                hs_count[0] += 16
                split(u0 + 10)
                hidden_split(10)
                split(u0 + 11)
                for n in range(KT):
                    dve.wait_ge(down_ready, down_base[s] + n + 1)
                    if s == "ffn2":
                        dve.tensor_copy(Y2[:, n, :], bank[n][:, :]).then_inc(down_added, 1)
                    else:
                        dve.tensor_tensor(X[:, n, :], X[:, n, :], bank[n][:, :], ALU.add).then_inc(down_added, 1)
                if s == "ffn2":
                    norm("fpost")

            def taps(i, c, half, t):
                dve.wait_ge(cv_act, i * 4 + (t + 1))
                dve.scalar_tensor_tensor(cv[:, t, 1:SEQ], bank[t][:, 0:SEQ - 1], V3(i, c, 1, half), cv[:, t, 1:SEQ],
                                         ALU.mult, ALU.add).then_inc(cv_one, 1)
                dve.wait_ge(cv_one, i * 4 + (t + 1))
                dve.scalar_tensor_tensor(cv[:, t, 2:SEQ], bank[t][:, 0:SEQ - 2], V3(i, c, 0, half), cv[:, t, 2:SEQ],
                                         ALU.mult, ALU.add).then_inc(cv_done, 1)

            def rope_table():
                rot = C("rotary")
                freq, phase, turn, sign = (rot[64:128, j:j + 1] for j in range(4))
                tab, pos, t0, t1 = rotab[64:128, :], posb[64:128, :], rtmp[64:128, 0, :], rtmp[64:128, 1, :]
                dve.wait_ge(pos_loaded, 16)
                link(dve.tensor_copy(tab, pos.bitcast(I32)))
                link(dve.tensor_scalar(tab, tab, freq, None, ALU.mult))
                link(dve.tensor_scalar(t0, tab, 1.0 / (2 * math.pi), turn, ALU.mult, ALU.add))
                link(dve.tensor_scalar(t0, t0, 12582912.0, 12582912.0, ALU.add, ALU.subtract))
                c1 = 6.28125
                c2 = 2029 / 2.0 ** 20
                c3 = 2 * math.pi - c1 - c2
                link(dve.scalar_tensor_tensor(tab, t0, -c1, tab, ALU.mult, ALU.add))
                link(dve.scalar_tensor_tensor(tab, t0, -c2, tab, ALU.mult, ALU.add))
                link(dve.scalar_tensor_tensor(tab, t0, -c3, tab, ALU.mult, ALU.add))
                link(dve.tensor_scalar(tab, tab, phase, 3.1415925, ALU.add, ALU.min))
                dve.tensor_scalar(tab, tab, -3.1415925, sign, ALU.max, ALU.mult).then_inc(rope_arg, 1)

            def mla():
                norm("mla")
                rope_table()
                L = lin_base["mla"]
                for u in tok_units("mla_down"):
                    split(u + 1)
                    for t in range(2):
                        j = 2 * (u - first["mla_down"]) + t
                        dve.wait_ge(lin_ready, L + 1)
                        b = bank[L % 4]
                        if j < 5:
                            dve.tensor_copy(cq[:, j, :], b[:, :]).then_inc(lin_free, 1)
                        else:
                            dve.wait_ge(rope_ready, 1)
                            dve.tensor_tensor(krope[64:96, :], b[64:96, :], rotab[64:96, :], ALU.mult)
                            dve.tensor_tensor(rtmp[64:96, 0, :], b[96:128, :], rotab[96:128, :],
                                              ALU.mult).then_inc(lin_free, 1)
                            dve.wait_ge(lin_free, L + 1)
                            dve.tensor_tensor(krope[64:96, :], krope[64:96, :], rtmp[64:96, 0, :],
                                              ALU.add).then_inc(krope_ready, 1)
                            dve.wait_ge(krope_ready, 1)
                        L += 1
                norm("q")
                norm("kv")
                for half in range(2):
                    for u in tok_units(f"mla_q{half}"):
                        split(u + 1)
                        for t in range(4):
                            h = 4 * (u - first[f"mla_q{half}"]) + t
                            dve.wait_ge(lin_ready, L + 1)
                            dve.wait_ge(lin_act, 12 * half + h + 1)
                            if 8 * half + h >= 2:
                                dve.wait_ge(rope_done, 8 * half + h - 1)
                            b = bank[L % 4]
                            dve.tensor_tensor(qc[64:96, h, :], b[64:96, :], rotab[64:96, :], ALU.mult)
                            dve.tensor_tensor(rtmp[64:96, h % 2, :], b[96:128, :], rotab[96:128, :],
                                              ALU.mult).then_inc(lin_free, 1)
                            L += 1
                    for u in tok_units(f"mla_kv{half}"):
                        split(u + 1)
                        for t in range(4):
                            dve.wait_ge(lin_ready, L + 1)
                            dve.wait_ge(lin_act, 12 * half + 8 + t + 1)
                            dve.tensor_copy(kc[0:64, 2 * t + 1, :], bank[L % 4][64:128, :]).then_inc(lin_free, 1)
                            L += 1
                        for t in range(4):
                            dve.wait_ge(lin_ready, L + 1)
                            dve.tensor_copy(vm[:, t, :], bank[L % 4][:, :]).then_inc(lin_free, 1)
                            L += 1
                    attention(f"mla{half}")
                head_pairs_out("mla", None)
                residual("mla_out", L)

            def mix2():
                norm("pre")
                L = lin_base["mix2"]
                dve.wait_ge(lam_loaded, 16)
                v = lamv[:, 0:256].rearrange("p (a b) -> p a b", b=64)
                dve.tensor_scalar(subg, V("diff_subln_2", 0), 1.0 - LAM_INIT, None, ALU.mult)
                link(dve.tensor_tensor(odt[:, 0, 0:64], v[:, 0, :], v[:, 1, :], ALU.mult))
                link(dve.tensor_tensor(odt[:, 1, 0:64], v[:, 2, :], v[:, 3, :], ALU.mult))
                dve.tensor_reduce(lam[:, 0:2], odt[:, 0:2, 0:64], AX.X, ALU.add).then_inc(lam_prod, 1)
                dve.wait_ge(lam_exp, 1)
                link(dve.scalar_tensor_tensor(lam[:, 2:3], lam[:, 0:1], LAM_INIT, lam[:, 1:2], ALU.add, ALU.subtract))
                dve.tensor_scalar(mu1, vec[:, vcol["mu_shift_2"]:vcol["mu_shift_2"] + 14], -1.0, 1.0, ALU.mult, ALU.add)
                link(dve.tensor_scalar(ka1, vec[:, vcol["k_a_2"]:vcol["k_a_2"] + 4], -1.0, 1.0, ALU.mult, ALU.add))
                acts = 24 if "mla" in stages else 0
                for u in tok_units("diff_in"):
                    split(u + 1)
                    j = u - first["diff_in"]
                    if j < 4:
                        for t in range(2):
                            h = 2 * (j % 2) + t
                            acts += 1
                            dve.wait_ge(lin_ready, L + 1)
                            dve.wait_ge(lin_act, acts)
                            dve.tensor_copy((qd, kd)[j // 2][0:64, 2 * h + 1, :], bank[L % 4][64:128, :])\
                                .then_inc(lin_free, 1)
                            L += 1
                    else:
                        for t in range(4):
                            dve.wait_ge(lin_ready, L + 1)
                            dve.tensor_copy(vd[:, t, 256 * (j - 4):256 * (j - 3)], bank[L % 4][:, 0:256])\
                                .then_inc(lin_free, 1)
                            L += 1
                attention("diff")
                dve.wait_ge(sub_rstd, 1)
                for h in range(4):
                    o = otok_d[:, :, 128 * h:128 * h + 128]
                    dve.tensor_tensor(o, o, ssd[:, 4 * h:4 * h + 4].unsqueeze(2).broadcast_to([P, 4, P]),
                                      ALU.mult).then_inc(ot_ready, 1)
                for u in tok_units("rwkv_in"):
                    split(u + 1)
                    for t in range(2):
                        j = 2 * (u - first["rwkv_in"]) + t
                        acts += 1
                        dve.wait_ge(lin_act, acts)
                        to = rwkv_tile(j)
                        dve.scalar_tensor_tensor(to[:, 1:SEQ], bank[L % 4][:, 0:SEQ - 1], V("mu_shift_2", j),
                                                 to[:, 1:SEQ], ALU.mult, ALU.add).then_inc(lin_free, 1)
                        L += 1
                head_pairs_out("mix2", subg)
                rwkv_prepare()
                rwkv_chunks()
                group_norm()
                for u in tok_units("mix_out"):
                    split(u + 1)
                    for t in range(2):
                        n = 2 * (u - first["mix_out"]) + t
                        dve.wait_ge(lin_ready, L + 1)
                        dve.tensor_copy(Y2[:, n, :], bank[L % 4][:, :]).then_inc(lin_free, 1)
                        L += 1
                norm("post")

            def rwkv_prepare():
                for t in range(4):
                    r, k, v, a = rr[:, t, :], kk[:, t, :], vv[:, t, :], aa[:, t, :]
                    dve.wait_ge(rw_sig, 2 * t + 2)
                    link(dve.tensor_scalar(RT[:, 0, :], k, V("k_k_2", t), None, ALU.mult))
                    dve.tensor_tensor(RT[:, 1, :], RT[:, 0, :], RT[:, 0, :], ALU.mult).then_inc(rw_sqs, 1)
                    link(dve.tensor_scalar(RT[:, 3, :], a, V("k_a_2", t), ka1[:, t:t + 1], ALU.mult, ALU.add))
                    link(dve.tensor_tensor(k, k, RT[:, 3, :], ALU.mult))
                    dve.scalar_tensor_tensor(RT[:, 2, :], r, V("r_k_2", t), k, ALU.mult, ALU.mult).then_inc(rw_sqs, 1)
                    for n in range(NCH):
                        last = dve.tensor_tensor_scan(RT[:, 4, chunk(n)], C("ones"), sgw[:, t, chunk(n)], 0.0,
                                                      ALU.mult, ALU.add)
                    link(last)
                    cs = RT[:, 4, :].rearrange("p (n c) -> p n c", c=CH)
                    link(dve.tensor_copy(cmid[:, t, :].unsqueeze(2), cs[:, :, 63:64]))
                    link(dve.tensor_tensor(cs, cs, cmid[:, t, :].unsqueeze(2).broadcast_to([P, NCH, CH]), ALU.subtract))
                    dve.tensor_copy(cend[:, t, :].unsqueeze(2), cs[:, :, CH - 1:CH])
                    dve.tensor_tensor(RT[:, 3, :], RT[:, 4, :], sgw[:, t, :], ALU.subtract).then_inc(rw_d, 1)
                    dve.wait_ge(rw_sum, 2 * t + 1)
                    dve.tensor_scalar(RT[:, 1, :], bank[4][:, :], 1e-24, None, ALU.max).then_inc(rw_max, 1)
                    dve.wait_ge(rw_vt, t + 1)
                    dve.wait_ge(rw_sum, 2 * t + 2)
                    dve.tensor_tensor(v, v, bank[5][:, :], ALU.mult).then_inc(rw_bonus, 1)
                    dve.wait_ge(rw_exp, t + 1)
                    kr = KR[:, t, :, :]
                    split3 = lambda x: x.rearrange("p (n c) -> p n c", c=CH)
                    dve.tensor_tensor(kr[:, :, CH:2 * CH], split3(r), split3(RT[:, 4, :]), ALU.mult)
                    dve.tensor_tensor(k, k, RT[:, 2, :], ALU.mult)
                    dve.wait_ge(rw_rn, t + 1)
                    link(dve.tensor_tensor(RT[:, 0, :], RT[:, 0, :], RT[:, 1, :], ALU.mult))
                    link(dve.tensor_tensor(a, a, RT[:, 0, :], ALU.mult))
                    dve.tensor_tensor(kr[:, :, 0:CH], split3(RT[:, 0, :]), split3(RT[:, 3, :]), ALU.mult)
                    link(dve.tensor_tensor(a, a, RT[:, 2, :], ALU.mult))
                dve.tensor_tensor(facl[:, :, 0:3], cend[:, :, 0:3], cmid[:, :, 1:4], ALU.add).then_inc(rw_facl, 1)
                link(dve.memset(STt, 0.0))
                dve.wait_ge(rw_fac, 1)

            def rwkv_chunks():
                for n in range(NCH):
                    for h in range(8):
                        dve.wait_ge(rw_a, 8 * n + h + 1)
                        dve.tensor_tensor(AM[:, h, :], bank[h % 4][:, :], C("pair_masks"), ALU.mult).then_inc(rw_am, 1)
                    for g in range(2):
                        x = XiT[:, g, :].rearrange("p (h n) -> p h n", n=P)
                        if g == 0:
                            dve.wait_ge(rw_am, 8 * n + 8)
                        lv = C("level0").unsqueeze(1).broadcast_to([P, 4, P])
                        link(dve.tensor_tensor(x, AM[:, 4 * g:4 * g + 4, 0:128], lv, ALU.mult))
                        dve.tensor_tensor(x, x, ident.unsqueeze(1).broadcast_to([P, 4, P]), ALU.add).then_inc(rw_xt0, 1)
                    for level in range(1, LEVELS):
                        for g in range(2):
                            at = (n * (LEVELS - 1) + level - 1) * 2 + g
                            dve.wait_ge(rw_xx, at + 1)
                            for part, x in enumerate((XiT, Xi)):
                                if part == 0 or level < LEVELS - 1:
                                    to = half_blocks(x[:, g, :], level, 1 - part)
                                    new = bank[2 + 2 * part + g][:, 0:256].rearrange("p (b c) -> p b c", c=1 << level)
                                    last = dve.tensor_tensor(to, to, new, ALU.add)
                            last.then_inc(rw_xn, 1)
                    dve.wait_ge(rw_y, n + 1)
                    y = vv[:, :, chunk(n)]
                    dve.tensor_tensor(y, y, bank[2][:, :].rearrange("p (t c) -> p t c", c=CH), ALU.add).then_inc(rw_yc, 1)
                    dve.wait_ge(rw_s, n + 1)
                    s3 = bank[3][:, 0:256].rearrange("p (t v) -> p t v", v=64)
                    link(dve.tensor_tensor(STt, STt, s3, ALU.add))
                    if n < NCH - 1:
                        f = fac[:, :, n:n + 1].broadcast_to([P, 4, 64])
                        dve.tensor_tensor(STt, STt, f, ALU.mult).then_inc(rw_st, 1)

            def group_norm():
                def centre(t):
                    y = vv[:, t, :]
                    dve.wait_ge(gn_mean, t + 1)
                    link(dve.scalar_tensor_tensor(y, bank[GN[t % 2][0]][:, :], -1.0 / 64, y, ALU.mult, ALU.add))
                    dve.tensor_tensor(NS[:, t % 2, :], y, y, ALU.mult).then_inc(gn_cent, 1)

                def finish(t):
                    y = vv[:, t, :]
                    dve.wait_ge(gn_rstd, t + 1)
                    link(dve.tensor_tensor(y, y, XiT[:, t % 2, :], ALU.mult))
                    link(dve.tensor_scalar(y, y, V("ln_x_w_2", t), V("ln_x_b_2", t), ALU.mult, ALU.add))
                    dve.wait_ge(gn_gate, t + 1)
                    dve.tensor_tensor(Xi[:, t % 2, :], y, bank[GN[t % 2][2]][:, :], ALU.mult).then_inc(gn_out, 1)

                def low(t):
                    dve.wait_ge(gn_hi, t + 1)
                    dve.tensor_tensor(XL[:, t, :], Xi[:, t % 2, :], XH[:, t, :].bitcast(F32), ALU.subtract)\
                       .then_inc(gn_lo, 1)

                dve.wait_ge(rw_yc, NCH)
                centre(0)
                for t in range(4):
                    if t < 3:
                        centre(t + 1)
                    finish(t)
                    if t >= 1:
                        low(t - 1)
                low(3)

            dve.memset(epsb[:, 0:1], EPS)
            dve.memset(epsb[:, 1:2], SUBLN_EPS)
            dve.memset(epsb[:, 2:3], 15 * math.log(2.0))
            dve.memset(epsb[:, 3:4], RWKV_LN_EPS)
            dve.wait_ge(setup_loaded, 32)
            dve.tensor_copy(identR[:, :], ident).then_inc(setup_ready, 1)
            dve.wait_ge(turned, 1)
            dve.tensor_copy(vec[:, :], bank[0][:, 0:3 * P]).then_inc(turned_out, 1)
            for f in range(KT):
                dve.wait_ge(turned, f + 2)
                dve.tensor_copy(X[:, f, :], bank[1 + f % 2][:, :]).then_inc(turned_out, 1)
            dve.wait_ge(consts_loaded, 16)
            dve.tensor_copy(masks[:, 0, :], C("mask_qk"))
            dve.tensor_copy(masks[:, 1, :], C("mask_kq")).then_inc(setup_ready, 1)
            if "even" in stages:
                dve.wait_ge(side_loaded, 32)
                dve.memset(tabx[32:33, :], 1.0).then_inc(bias_row, 1)
            dve.wait_ge(turned_out, 9)
            split(0)
            if "even" in stages:
                dve.wait_ge(bias_turned, 1)
                dve.tensor_copy(brow[0:8, 0:384], bank[3][0:8, 0:384]).then_inc(bias_row_ready, 1)
            for s in stages:
                {"even": even, "mla": mla, "mix2": mix2, "fnorm": lambda: norm("fnorm")}.get(s, lambda: ffn(s))()
            for n in range(2 * ST):
                dve.wait_ge(turned, 9 + n + 1)
                dve.tensor_copy(xtok[:, n // 2, 512 * (n % 2):512 * (n % 2) + 512], bank[1 + n % 2][:, :])\
                   .then_inc(turned_out, 1)

        @block.tensor
        def _(pe):
            def sum_squares(name):
                use, t0, tiles, src, col, gain, done = norm_plan(name)
                if use:
                    pe.wait_ge(rstd_ready, use)
                for k in range(tiles):
                    pe.wait_ge(sq_ready, t0 + k + 1)
                    pe.matmul(bank[7][:, :], C("ones"), NS[:, k % 2, :], start=(k == 0), stop=(k == tiles - 1))\
                      .then_inc(sq_used, 1)

            def feature_tile(u, kt, n, cols, M, x0, L, first_k=True, last_k=True, norm=None):
                hi, lo = wv(u, n, kt)
                for k in range(kt):
                    if norm is not None:
                        pe.wait_ge(*low_ready(norm, k))
                    for j, (w, x) in enumerate(((hi, XH), (hi, XL), (lo, XH))):
                        m = pe.matmul(bank[L % 4][0:M, :], cols(w, k), x[:, x0 + k, :],
                                      start=(first_k and k == 0 and j == 0), stop=(last_k and k == kt - 1 and j == 2))
                return m

            def token_tile(u, kt, n, cols, N, x0, s, L):
                hi, lo = wv(u, n, kt)
                for k in range(kt):
                    for j, (w, x) in enumerate(((hi, XH), (hi, XL), (lo, XH))):
                        m = pe.matmul(bank[L % 4][:, 0:N], x[:, x0 + k, s * P:(s + 1) * P], cols(w, k),
                                      start=(k == 0 and j == 0), stop=(k == kt - 1 and j == 2))
                return m

            def free(L):
                if L >= 4:
                    pe.wait_ge(lin_free, L - 3)

            def unit(u):
                pe.wait_ge(w_lo_ready, u + 1)

            def whole(c0):
                return lambda w, k: w[:, k, c0:c0 + P]

            def linear(stage, L):
                for u in tok_units(stage):
                    unit(u)
                    for t in range(2):
                        free(L)
                        m = feature_tile(u, KT, 256, whole(P * t), P, 0, L)
                        m.then_inc(lin_ready, 1)
                        L += 1
                    tick(u)
                return L

            def tick(u):
                pe.matmul(bank[6][:, 0:2], identR[:, :], identR[:, 0:2], start=True, stop=True).then_inc(w_used, 1)

            def turn_pairs(s, otok, ready):
                for t in range(OT_TILES[s]):
                    pe.wait_ge(*ready(t))
                    if t >= 2:
                        pe.wait_ge(ot_lo, ot_base[s] + t - 1)
                    for i in range(ST):
                        m = pe.transpose(bank[t % 2][:, P * i:P * (i + 1)], otok[:, i, P * t:P * (t + 1)], ident)
                    m.then_inc(ot_turned, 1)
                pe.wait_ge(ot_lo, ot_base[s] + OT_TILES[s])

            def attention(name):
                A = ATT[name]
                groups, g0, h0 = A["list"], A["g0"], A["h0"]
                q, k, v, dv = A["q"], A["k"], A["v"], A["dv"]

                def scores(n):
                    g = g0 + n
                    h, gi, tiles = groups[n]
                    if n >= 3:
                        pe.wait_ge(at_p, g - 2)
                    for i, k0, nk, c in tiles:
                        m = pe.matmul(bank[g % 3][:, c:c + P * nk], q(h)[:, P * i:P * (i + 1)],
                                      k(h)[:, P * k0:P * (k0 + nk)], start=True, stop=True)
                        if A["mask"]:
                            m = pe.matmul(bank[g % 3][:, c + P * (nk - 1):c + P * nk], identR[:, :], masks[:, 0, :],
                                          start=False, stop=True, skip_group_check=True)
                    m.then_inc(at_s, 1)

                def turn(n):
                    g = g0 + n
                    h, gi, tiles = groups[n]
                    pe.wait_ge(at_p, g + 1)
                    if g >= 2:
                        pe.wait_ge(at_pt, g - 1)
                    for i, k0, nk, c in tiles:
                        for j in range(nk):
                            s = slice(c + P * j, c + P * (j + 1))
                            m = pe.transpose(bank[3 + g % 2][:, s], Pb[:, g % 3, s], ident)
                    m.then_inc(at_t, 1)

                def values(n):
                    g = g0 + n
                    h, gi, tiles = groups[n]
                    hh = h0 + h
                    pe.wait_ge(at_pt, g + 1)
                    if gi == 0 and hh >= 2:
                        pe.wait_ge(at_on, hh - 1)
                    for i, k0, nk, c in tiles:
                        for j in range(nk):
                            m = pe.matmul(bank[5 + hh % 2][:, dv * i:dv * (i + 1)], PTb[:, g % 2, c + P * j:c + P * (j + 1)],
                                          v(h, k0 + j), start=(j == 0), stop=(j == nk - 1))
                    m.then_inc(at_o, 1)

                N = len(groups)
                scores(0)
                scores(1)
                for n in range(N):
                    if n + 2 < N:
                        scores(n + 2)
                    turn(n)
                    if n >= 1:
                        values(n - 1)
                values(N - 1)
                pe.wait_ge(at_on, h0 + 8)

            def stick_breaking():
                def z(h):
                    b = base_of(h)
                    t = h // 2
                    if h >= 2:
                        pe.wait_ge(sb_w, h - 1)
                    for j in (0, 1, 3, 2):
                        bk, c = SBANK[j]
                        o = bank[3 * (h % 2) + bk]
                        pe.matmul(o[:, c:c + SEQ - P * j], kTa[b:b + 64, t, P * j:P * (j + 1)],
                                  qTa[b:b + 64, t, P * j:SEQ], start=(j != 3), stop=True, skip_group_check=True)
                        m = pe.matmul(o[:, c:c + P], identR[:, :], masks[:, 1, :], start=False, stop=True,
                                      skip_group_check=True)
                    m.then_inc(sb_z, 1)

                def suffix(h):
                    pe.wait_ge(sb_sp, h + 1)
                    for j in (0, 1, 3, 2):
                        bk, c = SBANK[j]
                        o = bank[3 * (h % 2) + bk]
                        for e in range(j, 4):
                            m = pe.matmul(o[:, c + P * (e - j):c + SEQ - P * j], C("neg_suffix" if e == j else "neg_ones"),
                                          SBL[:, h % 3, SBOFF[e]:SBOFF[e] + SEQ - P * e], start=False, stop=True,
                                          skip_group_check=True)
                    m.then_inc(sb_sum, 1)

                def values(h):
                    b, t = base_of(h), h // 2
                    pe.wait_ge(sb_w, h + 1)
                    if h % 2 == 0 and t >= 2:
                        pe.wait_ge(sb_olo, t - 1)
                    for j in range(4):
                        m = pe.matmul(bank[6 + t % 2][b:b + 64, P * j:SEQ], va[:, j, 64 * h:64 * h + 64],
                                      SBL[:, h % 3, SBOFF[j]:SBOFF[j] + SEQ - P * j], start=(j == 0), stop=(j == 3))
                    m.then_inc(sb_o, 1)

                z(0)
                z(1)
                for h in range(8):
                    suffix(h)
                    if h >= 1:
                        values(h - 1)
                    if h + 2 < 8:
                        z(h + 2)
                values(7)

            def even():
                sum_squares("even")
                pe.wait_ge(bias_row_ready, 1)
                L = lin_base["even"]
                for u in tok_units("even_qkv"):
                    j = u - first["even_qkv"]
                    unit(u)
                    for t in range(2 if j < 4 else 4):
                        free(L)
                        if j < 4:
                            m = feature_tile(u, KT, 256, whole(P * t), P, 0, L,
                                             norm="even" if j == 0 and t == 0 else None)
                        else:
                            m = token_tile(u, KT, 256, lambda w, k: w[:, k, :], 256, 0, t, L)
                        m.then_inc(lin_ready, 1)
                        L += 1
                    tick(u)
                for part, u in enumerate(tok_units("even_qb")):
                    unit(u)
                    for t in range(4):
                        if part == 0:
                            free(L + t)
                        m = feature_tile(u, 4, 512, whole(P * t), P, 4 * part, L + t, first_k=(part == 0), last_k=(part == 1))
                        if part == 1:
                            m.then_inc(lin_ready, 1)
                    tick(u)
                L += 4
                u = tok_units("even_kvb")[0]
                unit(u)
                free(L)
                feature_tile(u, KT, 256, whole(0), P, 0, L).then_inc(lin_ready, 1)
                L += 1
                for t in range(4):
                    free(L)
                    token_tile(u, KT, 256, whole(P), P, 0, t, L).then_inc(lin_ready, 1)
                    L += 1
                tick(u)
                pe.wait_ge(lin_free, L)
                pe.wait_ge(bias_back, 128)
                for j in range(4):
                    pe.matmul(bank[3 + j][:, :], C("flip"), winrev[:, 2 * j:2 * j + 2, :], start=True, stop=True)\
                      .then_inc(bias_turned, 1)
                pe.wait_ge(winbias_ready, 4)
                stick_breaking()
                pe.wait_ge(sb_olo, 4)
                attention("win")
                turn_pairs("even", otok_e, lambda t: (at_on, ATT["win"]["h0"] + 8))
                linear("even_out", L)

            def ffn(s):
                name = s if s != "ffn2" else "fpre"
                sum_squares(name)
                u0, h0 = first[s + "_up"], hid_base[s]
                def body(i):
                    for part in range(2):
                        pe.wait_ge(w_lo_ready, i * 2 + (u0 + part + 1))
                        for c in range(2):
                            b = 2 * part + c
                            if c == 0 and not (isinstance(i, int) and h0 == 0):
                                if s == "ffn2" and not isinstance(i, int):
                                    pe.wait_ge(cv_done, i * 4 + (2 * part - 2))
                                else:
                                    pe.wait_ge(silu_done if s != "ffn2" and part == 0 else hid_done, i * 2 + h0)
                            hi, lo = wv(u0 + part, 256, KT)
                            for k in range(KT):
                                if isinstance(i, int) and part == 0 and c == 0:
                                    pe.wait_ge(*low_ready(name, k))
                                for j, (w, x) in enumerate(((hi, XH), (hi, XL), (lo, XH))):
                                    m = pe.matmul(bank[b][:, :], w[:, k, P * c:P * (c + 1)], x[:, k, :],
                                                  start=(k == 0 and j == 0), stop=(k == KT - 1 and j == 2))
                            m.then_inc(g_ready if part == 0 else u_ready, 1)
                        tick(0)
                body(0)
                with pe.Fori(1, HT // 2) as i:
                    body(i)
                u0 = first[s + "_down"]
                pe.wait_ge(hid_done, h0 + HT)
                pe.wait_ge(silu_done, h0 + HT)

                def down_unit(slot, start, stop, ready):
                    hi, lo = wv(slot, D, 2)
                    for c in range(2):
                        if c == 0:
                            ready()
                        for n in range(KT):
                            for j, (w, a) in enumerate(((hi, XH), (hi, XL), (lo, XH))):
                                m = pe.matmul(bank[n][:, :], w[:, c, P * n:P * (n + 1)], a[:, (hslot[0] + c) % 4, :],
                                              start=(start and c == 0 and j == 0), stop=(stop and c == 1 and j == 2))
                            if stop and c == 1:
                                m.then_inc(down_ready, 1)
                    if not stop:
                        m.then_inc(w_used, 1)
                    hslot[0] = (hslot[0] + 2) % 4

                hslot = [0]

                def ready_at(j):
                    def wait():
                        pe.wait_ge(w_lo_ready, u0 + j + 1)
                        pe.wait_ge(hs_lo, h0 + 2 * j + 2)
                    return wait

                down_unit(u0, True, False, ready_at(0))
                down_unit(u0 + 1, False, False, ready_at(1))
                with pe.Fori(0, 4) as i:
                    for c in range(2):
                        def wait(c=c):
                            pe.wait_ge(w_lo_ready, i * 2 + (u0 + 3 + c))
                            pe.wait_ge(hs_lo, i * 4 + (h0 + 4 + 2 * c + 2))
                        down_unit(u0 + c, False, False, wait)
                down_unit(u0 + 10, False, True, ready_at(10))
                pe.wait_ge(down_added, down_base[s] + KT)
                tick(0)
                if s == "ffn2":
                    sum_squares("fpost")

            def mla():
                sum_squares("mla")
                L = lin_base["mla"]
                for u in tok_units("mla_down"):
                    unit(u)
                    j = u - first["mla_down"]
                    for t in range(2):
                        free(L)
                        if j < 2:
                            m = feature_tile(u, KT, 256, whole(P * t), P, 0, L,
                                             norm="mla" if j == 0 and t == 0 else None)
                        else:
                            m = feature_tile(u, KT, 192, whole(64 * t), P, 0, L)
                        m.then_inc(lin_ready, 1)
                        L += 1
                    tick(u)
                sum_squares("q")
                sum_squares("kv")
                for half in range(2):
                    for u in tok_units(f"mla_q{half}"):
                        unit(u)
                        for t in range(4):
                            free(L)
                            norm = "q" if half == 0 and u == first["mla_q0"] and t == 0 else None
                            feature_tile(u, 3, 512, whole(P * t), P, 0, L, norm=norm).then_inc(lin_ready, 1)
                            L += 1
                        tick(u)
                    for u in tok_units(f"mla_kv{half}"):
                        unit(u)
                        for t in range(4):
                            free(L)
                            norm = "kv" if half == 0 and t == 0 else None
                            feature_tile(u, 2, D, whole(P * t), P, 3, L, norm=norm).then_inc(lin_ready, 1)
                            L += 1
                        for t in range(4):
                            free(L)
                            token_tile(u, 2, D, lambda w, k: w[:, k, 512:1024], 512, 3, t, L)\
                                .then_inc(lin_ready, 1)
                            L += 1
                        tick(u)
                    pe.wait_ge(lin_free, L)
                    pe.wait_ge(rope_done, 8 * half + 8)
                    pe.wait_ge(krope_spread, 1)
                    attention(f"mla{half}")
                    if half == 0:
                        pe.wait_ge(at_p, ATT["mla0"]["g0"] + len(ATT["mla0"]["list"]))
                turn_pairs("mla", otok_m, lambda t: (at_on, ATT["mla1"]["h0"] + 8))
                linear("mla_out", L)

            def mix2():
                sum_squares("pre")
                L = lin_base["mix2"]
                for u in tok_units("diff_in"):
                    j = u - first["diff_in"]
                    unit(u)
                    for t in range(2 if j < 4 else 4):
                        free(L)
                        if j < 4:
                            m = feature_tile(u, KT, 256, whole(P * t), P, 0, L,
                                             norm="pre" if j == 0 and t == 0 else None)
                        else:
                            m = token_tile(u, KT, 256, lambda w, k: w[:, k, :], 256, 0, t, L)
                        m.then_inc(lin_ready, 1)
                        L += 1
                    tick(u)
                pe.wait_ge(lin_free, L)
                pe.wait_ge(alibi_loaded, 16 * 16)
                attention("diff")
                pe.wait_ge(at_p, ATT["diff"]["g0"] + len(ATT["diff"]["list"]))
                L = linear("rwkv_in", L)
                pe.wait_ge(lin_free, L)
                turn_pairs("mix2", otok_d, lambda t: (ot_ready, t + 1))
                rwkv_prepare()
                rwkv_chunks()
                group_norm()
                linear("mix_out", L)
                sum_squares("post")

            def rwkv_prepare():
                pe.wait_ge(rw_lora, 1)
                pe.wait_ge(wup_loaded, 48)
                for t in range(4):
                    for part in range(2):
                        if t >= 2:
                            pe.wait_ge(rw_sig, 2 * (t - 2) + part + 1)
                        r = slice(64 * part, 64 * part + 64)
                        pe.matmul(bank[2 + (2 * t + part) % 4][:, :], wup[r, 0, P * t:P * (t + 1)], lora[r, 0, :],
                                  start=True, stop=True).then_inc(rw_pre, 1)
                pe.wait_ge(rw_sig, 8)
                for t in range(4):
                    for part in range(2):
                        pe.wait_ge(rw_sqs, 2 * t + part + 1)
                        if t >= 1:
                            pe.wait_ge(rw_bonus if part else rw_max, t)
                        pe.matmul(bank[4 + part][:, :], C("half_ones"), RT[:, 1 + part, :], start=True, stop=True)\
                          .then_inc(rw_sum, 1)
                    if t >= 1:
                        pe.wait_ge(rw_vtok, t)
                    for n in range(NCH):
                        m = pe.transpose(bank[6][:, P * n:P * (n + 1)], vv[:, t, chunk(n)], ident)
                    m.then_inc(rw_vt, 1)
                pe.wait_ge(rw_fac, 1)
                pe.wait_ge(rw_vtok, 4)

            def rwkv_chunks():
                for n in range(NCH):
                    for part, src in enumerate((aa, kk)):
                        if n >= 1:
                            pe.wait_ge(rw_btc, 2 * n)
                        for t in range(4):
                            m = pe.transpose(bank[6 + part][:, P * t:P * (t + 1)], src[:, t, chunk(n)], ident)
                        m.then_inc(rw_bt, 1)
                    if n >= 1:
                        pe.wait_ge(rw_st, n)
                    for h in range(8):
                        b, t = base_of(h), h // 2
                        if h >= 4:
                            pe.wait_ge(rw_am, 8 * n + h - 3)
                        r = slice(b, b + 64)
                        pe.matmul(bank[h % 4][:, 0:256], aa[r, t, chunk(n)], KR[r, t, n, :], start=True, stop=True)
                        pe.matmul(bank[h % 4][:, 256:512], kk[r, t, chunk(n)], KR[r, t, n, :], start=True, stop=True)\
                          .then_inc(rw_a, 1)
                    for g in range(2):
                        pe.wait_ge(rw_xt0, 2 * n + g + 1)
                        for h in range(4):
                            s = slice(P * h, P * (h + 1))
                            m = pe.transpose(bank[4 + g][:, s], XiT[:, g, s], ident)
                        m.then_inc(rw_x0, 1)
                    for level in range(1, LEVELS):
                        last_level = level == LEVELS - 1

                        def t_part(g):
                            at = (n * (LEVELS - 1) + level - 1) * 2 + g
                            pe.wait_ge(rw_lvl, at + 1)
                            if level == 1:
                                pe.wait_ge(rw_x0c, 2 * n + g + 1)
                            else:
                                pe.wait_ge(rw_xn, at - 1)
                            for h in range(4):
                                s = slice(P * h, P * (h + 1))
                                m = pe.matmul(bank[g][:, s], Al[:, g, s], Xi[:, g, s], start=True, stop=True)
                            m.then_inc(rw_t, 1)

                        def x_part(g):
                            at = (n * (LEVELS - 1) + level - 1) * 2 + g
                            pe.wait_ge(rw_tc, at + 1)
                            for h in range(4):
                                s = slice(P * h, P * (h + 1))
                                m = pe.matmul(bank[2 + g][:, 64 * h:64 * h + 64], Tl[:, g, s],
                                              half_blocks(XiT[:, g, s], level, 1), start=True, stop=True)
                            if not last_level:
                                for h in range(4):
                                    s = slice(P * h, P * (h + 1))
                                    m = pe.matmul(bank[4 + g][:, 64 * h:64 * h + 64], XiT[:, g, s],
                                                  half_blocks(Tl[:, g, s], level, 0), start=True, stop=True)
                            m.then_inc(rw_xx, 1)

                        t_part(0)
                        t_part(1)
                        x_part(0)
                        x_part(1)
                    pe.wait_ge(rw_xn, (n + 1) * (LEVELS - 1) * 2)
                    for h in range(8):
                        b, t = base_of(h), h // 2
                        o = bank[h % 2][:, 64 * t:64 * t + 64]
                        pe.matmul(o, KR[b:b + 64, t, n, 0:CH], STt[b:b + 64, t, :], start=True, stop=False)
                        m = pe.matmul(o, AM[:, h, 256:384], vtok[:, n, 64 * h:64 * h + 64],
                                      start=False, stop=True)
                    m.then_inc(rw_p, 1)
                    pe.wait_ge(rw_pc, n + 1)
                    for h in range(8):
                        m = pe.matmul(bank[4][:, 64 * h:64 * h + 64], XiT[:, h // 4, P * (h % 4):P * (h % 4 + 1)],
                                      P0[:, 64 * h:64 * h + 64], start=True, stop=True)
                    m.then_inc(rw_u, 1)
                    pe.wait_ge(rw_uc, n + 1)
                    for h in range(8):
                        b, t = base_of(h), h // 2
                        o = bank[2][b:b + 64, P * t:P * (t + 1)]
                        hv = slice(64 * h, 64 * h + 64)
                        pe.matmul(o, P1[:, hv], AM[:, h, 128:256], start=True, stop=False)
                        pe.matmul(o, vtok[:, n, hv], AM[:, h, 384:512], start=False, stop=False)
                        m = pe.matmul(o, STt[b:b + 64, t, :], KR[b:b + 64, t, n, CH:2 * CH], start=False, stop=True)
                    m.then_inc(rw_y, 1)
                    pe.wait_ge(rw_btc, 2 * n + 2)
                    for h in range(8):
                        b, t = base_of(h), h // 2
                        o = bank[3][b:b + 64, 64 * t:64 * t + 64]
                        hv = slice(64 * h, 64 * h + 64)
                        c = slice(P * t + b, P * t + b + 64)
                        pe.matmul(o, BK[:, 0, c], P1[:, hv], start=True, stop=False)
                        m = pe.matmul(o, BK[:, 1, c], vtok[:, n, hv], start=False, stop=True)
                    m.then_inc(rw_s, 1)

            def group_norm():
                def mean_and_gate(t):
                    if t >= 2:
                        pe.wait_ge(gn_out, t - 1)
                    pe.matmul(bank[GN[t % 2][0]][:, :], C("half_ones"), vv[:, t, :], start=True, stop=True)\
                      .then_inc(gn_mean, 1)
                    pe.matmul(bank[GN[t % 2][2]][:, :], wup[:, 1, P * t:P * (t + 1)], lora[:, 1, :],
                              start=True, stop=True).then_inc(gn_gate, 1)

                pe.wait_ge(rw_yc, NCH)
                mean_and_gate(0)
                for t in range(4):
                    if t < 3:
                        mean_and_gate(t + 1)
                    pe.wait_ge(gn_cent, t + 1)
                    pe.matmul(bank[GN[t % 2][1]][:, :], C("half_ones"), NS[:, t % 2, :], start=True, stop=True)\
                      .then_inc(gn_var, 1)
                pe.wait_ge(gn_lo, 4)

            pe.wait_ge(setup_loaded, 32)
            for j in range(3):
                m = pe.transpose(bank[0][:, P * j:P * (j + 1)], vrow[:, j, :], ident)
            m.then_inc(turned, 1)
            pe.wait_ge(x_loaded, 16)
            for f in range(KT):
                if f >= 2:
                    pe.wait_ge(turned_out, f)
                for i in range(ST):
                    m = pe.transpose(bank[1 + f % 2][:, P * i:P * (i + 1)], xtok[:, i, P * f:P * (f + 1)], ident)
                m.then_inc(turned, 1)
            pe.wait_ge(setup_ready, 2)
            pe.wait_ge(turned_out, 9)
            if "even" in stages:
                pe.wait_ge(side_loaded, 32)
                pe.wait_ge(bias_row, 1)
                pe.matmul(bank[3][0:8, 0:384], tabx, C("buckets")[0:33, :], start=True, stop=True).then_inc(bias_turned, 1)
            for s in stages:
                {"even": even, "mla": mla, "mix2": mix2, "fnorm": lambda: sum_squares("fnorm")}.get(s, lambda: ffn(s))()
            fin, n0 = x_final["end"]
            pe.wait_ge(fin, n0 + KT)
            for n in range(2 * ST):
                if n >= 2:
                    pe.wait_ge(turned_out, 9 + n - 1)
                for c in range(4):
                    m = pe.transpose(bank[1 + n % 2][:, P * c:P * (c + 1)], X[:, 4 * (n % 2) + c, P * (n // 2):P * (n // 2 + 1)],
                                     ident)
                m.then_inc(turned, 1)


NAMES = ["x", "positions", "attn_norm", "ffn_norm", "even_w_in", "even_sinks", "even_w_out", "rel_bias_table",
         "mla_w_down", "mla_q_norm", "mla_w_uq", "mla_kv_norm", "mla_w_ukv", "mla_w_o", "ffn_w_gate", "ffn_w_up",
         "ffn_w_down", "final_norm", "w_in_2", "w_decay_up_2", "w_iclr_up_2", "w_gate_up_2", "w_out_2", "w_up_2",
         "w_down_2"]
LAMBDAS = ("lambda_q1_2", "lambda_k1_2", "lambda_q2_2", "lambda_k2_2")


def kernel(**inputs):
    import concourse.bacc as bacc
    from concourse.bass_utils import run_bass_kernel_spmd as run

    nc = bacc.Bacc("TRN2", target_bir_lowering=False, num_devices=1)
    arrays = {n: np.ascontiguousarray(inputs[n]) for n in NAMES}
    rows = [np.asarray(inputs[n]).reshape(-1, P) for n, _ in VECTORS]
    rows.append(np.zeros((3 * P - sum(r.shape[0] for r in rows), P), np.float32))
    arrays["vec_rows"] = np.concatenate(rows)
    arrays["lambdas"] = np.concatenate([np.asarray(inputs[n]).reshape(1, -1) for n in LAMBDAS], 1)
    arrays["const_cols"] = constants()
    arrays["alibi"] = alibi_rows()
    feeds, d = {}, {}
    for n, a in arrays.items():
        feeds["in_" + n] = a
        d[n] = nc.dram_tensor("in_" + n, a.shape, mybir.dt.from_np(a.dtype), kind="ExternalInput").ap()
    out = nc.dram_tensor("out", (1, SEQ, D), F32, kind="ExternalOutput").ap()
    scratch = nc.dram_tensor("bias_rows", (8, 384), F32, kind="Internal").ap()
    build(nc, d, out, scratch, STAGES)
    return run(nc, [feeds], core_ids=[0]).results[0]["out"]
```
